# Optimizing a Trainium2 kernel written in Bass

```python
import jax, jax.numpy as jnp
from jax import lax
import numpy as np

D_MODEL = 1024
BATCH = 1
SEQ = 128
DEPTH = 1
DEC_BATCH = 1
DEC_SEQ = 512
PAST_LEN = 256

GRID_W = 64
EPS = 1e-6
A_HEADS = 4
A_DK = 128
A_DV = 128
A_WIDTH = A_HEADS * A_DV
A_CHUNK = 16
B_HEADS = 8
B_KV_HEADS = 2
B_HEAD_DIM = 64
B_WIDTH = B_HEADS * B_HEAD_DIM
WINDOW = 128
B_BLOCK = 128
ROPE_BASE = 10000.0
P_HEADS = 8
P_NKEYS = 128
P_EXPERTS = P_NKEYS * P_NKEYS
P_QDIM = 256
P_TOPK = 16
P_TOK_BLOCK = 128
SEG_SIZES = (A_HEADS * A_DK, A_WIDTH, A_HEADS * A_DK, A_HEADS * A_DK, A_WIDTH,
             B_WIDTH, B_KV_HEADS * B_HEAD_DIM, B_KV_HEADS * B_HEAD_DIM, D_MODEL, D_MODEL)
D_IN = sum(SEG_SIZES)

kernel_name = 'hybrid_hgrn2_swa_peer_dit_step'

def rmsnorm(x, g):
    xf = x.astype(jnp.float32)
    y = xf * lax.rsqrt(jnp.mean(xf * xf, axis=-1, keepdims=True) + EPS)
    return (y * g.astype(jnp.float32)).astype(x.dtype)

def adaln(cond, w_ada, b_ada):
    m = (jax.nn.silu(cond) @ w_ada + b_ada)[:, None, :]
    return jnp.split(m, 6, axis=-1)

def split_columns(p):
    offs = np.cumsum(SEG_SIZES)[:-1].tolist()
    return jnp.split(p, offs, axis=-1)

def split_heads(x, h):
    return x.reshape(*x.shape[:-1], h, x.shape[-1] // h)

def axial_rope(x):
    T = x.shape[1]
    rows_n = T // GRID_W
    row = jnp.repeat(jnp.arange(rows_n), GRID_W).astype(jnp.float32)
    col = jnp.tile(jnp.arange(GRID_W), rows_n).astype(jnp.float32)
    half = x.shape[-1] // 2
    nf = half // 2
    inv = ROPE_BASE ** (-jnp.arange(nf, dtype=jnp.float32) / nf)

    def rot(xp, pos):
        ang = pos[:, None] * inv[None, :]
        cos = jnp.cos(ang)[None, :, None, :]
        sin = jnp.sin(ang)[None, :, None, :]
        x1 = xp[..., :nf].astype(jnp.float32)
        x2 = xp[..., nf:].astype(jnp.float32)
        return jnp.concatenate([x1 * cos - x2 * sin, x2 * cos + x1 * sin], axis=-1)

    return jnp.concatenate([rot(x[..., :half], row), rot(x[..., half:], col)], axis=-1).astype(x.dtype)

def hgrn2_chunk_scan(q, k, v, logf, s0):
    B_, T, H, DK = q.shape
    DV = v.shape[-1]
    C = A_CHUNK
    N = T // C
    f32 = jnp.float32

    def rs(a):
        return a.astype(f32).reshape(B_, N, C, H, a.shape[-1]).transpose(0, 3, 1, 2, 4)

    qc, kc, vc, gc = rs(q), rs(k), rs(v), rs(logf)
    bc = jnp.cumsum(gc, axis=3)
    causal = jnp.tril(jnp.ones((C, C), dtype=bool))
    diff = bc[:, :, :, :, None, :] - bc[:, :, :, None, :, :]
    decay = jnp.exp(jnp.where(causal[:, :, None], diff, -jnp.inf))
    scores = jnp.einsum('bhntk,bhnsk,bhntsk->bhnts', qc, kc, decay)
    o_intra = jnp.einsum('bhnts,bhnsv->bhntv', scores, vc)
    btot = bc[:, :, :, -1, :]
    k_end = kc * jnp.exp(btot[:, :, :, None, :] - bc)
    ds = jnp.einsum('bhnsk,bhnsv->bhnkv', k_end, vc)

    def step(s, inp):
        dec, d = inp
        return dec[..., None] * s + d, s

    s_final, s_start = lax.scan(step, s0.astype(f32),
                                (jnp.moveaxis(jnp.exp(btot), 2, 0), jnp.moveaxis(ds, 2, 0)))
    s_start = jnp.moveaxis(s_start, 0, 2)
    o_inter = jnp.einsum('bhntk,bhnkv->bhntv', qc * jnp.exp(bc), s_start)
    o = (o_intra + o_inter).transpose(0, 2, 3, 1, 4).reshape(B_, T, H, DV)
    return o, s_final

def hgrn2_mixer(aq, ai, af_f, af_b, ag, lb_f, lb_b, g_norm, s0_f, s0_b):
    B_, T, _ = aq.shape
    q = jax.nn.silu(split_heads(aq, A_HEADS))
    i = split_heads(ai, A_HEADS)

    def gates(af, lb):
        lbh = lb.reshape(A_HEADS, A_DK)
        f = lbh + (1.0 - lbh) * jax.nn.sigmoid(split_heads(af, A_HEADS).astype(jnp.float32))
        return 1.0 - f, jnp.log(f)

    k_f, lf_f = gates(af_f, lb_f)
    k_b, lf_b = gates(af_b, lb_b)
    o_f, s_f = hgrn2_chunk_scan(q, k_f, i, lf_f, s0_f)
    flip = lambda a: jnp.flip(a, axis=1)
    o_b, s_b = hgrn2_chunk_scan(flip(q), flip(k_b), flip(i), flip(lf_b), s0_b)
    o = o_f + flip(o_b)
    o = o * lax.rsqrt(jnp.mean(o * o, axis=-1, keepdims=True) + EPS)
    o = o * g_norm.astype(jnp.float32).reshape(A_HEADS, A_DV)
    o = o.reshape(B_, T, A_WIDTH).astype(ai.dtype) * jax.nn.silu(ag)
    return o, s_f, s_b

def context_attention(q, k, v, sink):
    B_, L, H, hd = q.shape
    KV = k.shape[2]
    G = H // KV
    nq = L // B_BLOCK
    scale = hd ** -0.5
    qb = q.reshape(B_, nq, B_BLOCK, KV, G, hd).transpose(1, 0, 2, 3, 4, 5)
    sink_col = sink.astype(jnp.float32).reshape(KV, G)

    def blk(qi):
        s = jnp.einsum('bqkgd,bskd->bkgqs', qi, k).astype(jnp.float32) * scale
        sc = jnp.broadcast_to(sink_col[None, :, :, None, None], s.shape[:-1] + (1,))
        p = jax.nn.softmax(jnp.concatenate([s, sc], axis=-1), axis=-1)[..., :-1]
        return jnp.einsum('bkgqs,bskd->bqkgd', p.astype(v.dtype), v)

    o = lax.map(blk, qb)
    return o.transpose(1, 0, 2, 3, 4, 5).reshape(B_, L, H * hd)

def latent_window_attention(q, k, v, ck, cv, sink):
    B_, T, H, hd = q.shape
    KV = k.shape[2]
    G = H // KV
    nb = T // B_BLOCK
    Lc = ck.shape[1]
    scale = hd ** -0.5
    qb = q.reshape(B_, nb, B_BLOCK, KV, G, hd)

    def band(a):
        ap = jnp.pad(a, ((0, 0), (B_BLOCK, B_BLOCK), (0, 0), (0, 0))).reshape(B_, nb + 2, B_BLOCK, KV, hd)
        return jnp.concatenate([ap[:, :-2], ap[:, 1:-1], ap[:, 2:]], axis=2)

    kw, vw = band(k), band(v)
    qpos = jnp.arange(nb)[:, None] * B_BLOCK + jnp.arange(B_BLOCK)[None, :]
    kpos = jnp.arange(nb)[:, None] * B_BLOCK + jnp.arange(3 * B_BLOCK)[None, :] - B_BLOCK
    kp = kpos[:, None, :]
    mask = (jnp.abs(kp - qpos[:, :, None]) <= WINDOW) & (kp >= 0) & (kp < T)
    s_loc = jnp.einsum('bnqkgd,bnskd->bkgnqs', qb, kw).astype(jnp.float32) * scale
    s_loc = jnp.where(mask, s_loc, -jnp.inf)
    s_ctx = jnp.einsum('bnqkgd,bskd->bkgnqs', qb, ck).astype(jnp.float32) * scale
    sc = jnp.broadcast_to(sink.astype(jnp.float32).reshape(KV, G)[None, :, :, None, None, None],
                          s_loc.shape[:-1] + (1,))
    p = jax.nn.softmax(jnp.concatenate([s_loc, s_ctx, sc], axis=-1), axis=-1).astype(v.dtype)
    o = (jnp.einsum('bkgnqs,bnskd->bnqkgd', p[..., :3 * B_BLOCK], vw)
         + jnp.einsum('bkgnqs,bskd->bnqkgd', p[..., 3 * B_BLOCK:3 * B_BLOCK + Lc], cv))
    return o.reshape(B_, T, H * hd)

def peer(h, w_q, sub_keys, w_u, w_v):
    B_, T, D = h.shape
    xs = h.reshape(-1, P_TOK_BLOCK, D)

    def per_block(xb):
        n = xb.shape[0]
        q = (xb @ w_q).reshape(n, P_HEADS, 2, P_QDIM // 2)
        s = jnp.einsum('nhpd,hpkd->nhpk', q, sub_keys).astype(jnp.float32)
        s1, i1 = lax.top_k(s[:, :, 0], P_TOPK)
        s2, i2 = lax.top_k(s[:, :, 1], P_TOPK)
        cand_s = (s1[..., :, None] + s2[..., None, :]).reshape(n, P_HEADS, P_TOPK * P_TOPK)
        cand_i = (i1[..., :, None] * P_NKEYS + i2[..., None, :]).reshape(n, P_HEADS, P_TOPK * P_TOPK)
        top_s, pos = lax.top_k(cand_s, P_TOPK)
        idx = jnp.take_along_axis(cand_i, pos, axis=-1)
        g = jax.nn.softmax(top_s, axis=-1)
        u = jnp.take(w_u, idx, axis=0)
        act = jax.nn.gelu(jnp.einsum('nhkd,nd->nhk', u, xb).astype(jnp.float32), approximate=False)
        v = jnp.take(w_v, idx, axis=0)
        return jnp.einsum('nhk,nhkd->nd', (g * act).astype(xb.dtype), v)

    return lax.map(per_block, xs).reshape(B_, T, D)

def trunk_layer(x, cond, w_ada, b_ada, g1, g2, w_in, lb_f, lb_b, a_norm, sink, w_oa, w_ob, w_out,
                p_wq, p_keys, p_u, p_v, s0_f, s0_b, ctx_k, ctx_v):
    sh1, sc1, gt1, sh2, sc2, gt2 = adaln(cond, w_ada, b_ada)
    h = rmsnorm(x, g1) * (1.0 + sc1) + sh1
    aq, ai, aff, afb, ag, bq, bk, bv, ga, gb = split_columns(h @ w_in)
    o_a, s_f, s_b = hgrn2_mixer(aq, ai, aff, afb, ag, lb_f, lb_b, a_norm, s0_f, s0_b)
    q = split_heads(bq, B_HEADS)
    k = split_heads(bk, B_KV_HEADS)
    v = split_heads(bv, B_KV_HEADS)
    if ctx_k is None:
        o_b = context_attention(q, k, v, sink)
    else:
        o_b = latent_window_attention(axial_rope(q), axial_rope(k), v, ctx_k, ctx_v, sink)
    y = (jax.nn.sigmoid(ga) * (o_a @ w_oa) + jax.nn.sigmoid(gb) * (o_b @ w_ob)) @ w_out
    x = x + gt1 * y
    h2 = rmsnorm(x, g2) * (1.0 + sc2) + sh2
    x = x + gt2 * peer(h2, p_wq, p_keys, p_u, p_v)
    return x, s_f, s_b, k, v

def setup_inputs(seed: int = 0) -> dict:
    key = jax.random.key(seed)
    ks = jax.random.split(key, 24)
    f32 = jnp.float32
    nrm = lambda k, shape, s: jax.random.normal(k, shape, f32) * s
    return {
        'x_prompt': nrm(ks[0], (BATCH, SEQ, D_MODEL), 1.0),
        'x_sample': nrm(ks[1], (DEC_BATCH, DEC_SEQ, D_MODEL), 1.0),
        'state_hgrn': nrm(ks[2], (DEC_BATCH, DEPTH, 2, A_HEADS, A_DK, A_DV), 0.5),
        'cache_k': nrm(ks[3], (DEC_BATCH, DEPTH, PAST_LEN, B_KV_HEADS, B_HEAD_DIM), 1.0),
        'cache_v': nrm(ks[4], (DEC_BATCH, DEPTH, PAST_LEN, B_KV_HEADS, B_HEAD_DIM), 1.0),
        'c': nrm(ks[5], (DEC_BATCH, D_MODEL), 1.0),
        'c_ctx': nrm(ks[6], (D_MODEL,), 1.0),
        'w_ada': nrm(ks[7], (DEPTH, D_MODEL, 6 * D_MODEL), 0.5 * D_MODEL ** -0.5),
        'b_ada': nrm(ks[8], (DEPTH, 6 * D_MODEL), 0.02),
        'norm1': 1.0 + nrm(ks[9], (DEPTH, D_MODEL), 0.02),
        'norm2': 1.0 + nrm(ks[10], (DEPTH, D_MODEL), 0.02),
        'w_in': nrm(ks[11], (DEPTH, D_MODEL, D_IN), D_MODEL ** -0.5),
        'lb_logits': nrm(ks[12], (2, DEPTH + 1, A_HEADS * A_DK), 0.1),
        'a_norm': 1.0 + nrm(ks[13], (DEPTH, A_WIDTH), 0.02),
        'b_sink': nrm(ks[14], (DEPTH, B_HEADS), 0.5),
        'w_oa': nrm(ks[15], (DEPTH, A_WIDTH, D_MODEL), A_WIDTH ** -0.5),
        'w_ob': nrm(ks[16], (DEPTH, B_WIDTH, D_MODEL), B_WIDTH ** -0.5),
        'w_out': nrm(ks[17], (DEPTH, D_MODEL, D_MODEL), D_MODEL ** -0.5),
        'p_wq': nrm(ks[18], (DEPTH, D_MODEL, P_HEADS * P_QDIM), D_MODEL ** -0.5),
        'p_keys': nrm(ks[19], (DEPTH, P_HEADS, 2, P_NKEYS, P_QDIM // 2), (P_QDIM // 2) ** -0.5),
        'p_u': nrm(ks[20], (DEPTH, P_EXPERTS, D_MODEL), D_MODEL ** -0.5),
        'p_v': nrm(ks[21], (DEPTH, P_EXPERTS, D_MODEL), P_HEADS ** -0.5),
        'norm_f': 1.0 + nrm(ks[22], (D_MODEL,), 0.02),
    }

def reference(x_prompt, x_sample, state_hgrn, cache_k, cache_v, c, c_ctx, w_ada, b_ada, norm1, norm2,
              w_in, lb_logits, a_norm, b_sink, w_oa, w_ob, w_out, p_wq, p_keys, p_u, p_v, norm_f):
    f32 = jnp.float32
    lb = jnp.cumsum(jax.nn.softmax(lb_logits.astype(f32), axis=1), axis=1)
    bp = x_prompt.shape[0]
    zeros = jnp.zeros((bp, A_HEADS, A_DK, A_DV), f32)
    xp, xs = x_prompt, x_sample
    states, kcs, vcs = [], [], []
    for l in range(DEPTH):
        lw = (w_ada[l], b_ada[l], norm1[l], norm2[l], w_in[l], lb[0, l], lb[1, l], a_norm[l], b_sink[l],
              w_oa[l], w_ob[l], w_out[l], p_wq[l], p_keys[l], p_u[l], p_v[l])
        xp, sf, sb, kc, vc = trunk_layer(xp, c_ctx[None, :], *lw, zeros, zeros, None, None)
        xs, _, _, _, _ = trunk_layer(xs, c, *lw, state_hgrn[:, l, 0].astype(f32),
                                     state_hgrn[:, l, 1].astype(f32), cache_k[:, l], cache_v[:, l])
        states.append(jnp.stack([sf, sb], axis=1).astype(x_prompt.dtype))
        kcs.append(kc)
        vcs.append(vc)
    y_prompt = rmsnorm(xp, norm_f)
    y_sample = rmsnorm(xs, norm_f)
    new_state_hgrn = jnp.stack(states, axis=1)
    new_cache_k = jnp.stack(kcs, axis=1)
    new_cache_v = jnp.stack(vcs, axis=1)
    return (y_prompt, y_sample, new_state_hgrn, new_cache_k, new_cache_v)


_drawn_inputs = setup_inputs


def setup_inputs(seed=0):
    import zlib

    import numpy as np

    out = dict(_drawn_inputs(seed))
    spreads = {}
    factors = {'state_hgrn': 8.0,
     'cache_k': 5.323,
     'cache_v': 4.664,
     'norm1': 2.897,
     'norm2': 19.645,
     'a_norm': 8.0,
     'b_sink': 64.0,
     'norm_f': 7.75}
    for name, (base, spread) in spreads.items():
        noise = np.random.default_rng([zlib.crc32(name.encode()), seed]).standard_normal(out[name].shape)
        drawn = base * np.exp(spread * noise) if base else spread * noise
        out[name] = __import__('jax').numpy.asarray(drawn.astype(out[name].dtype))
    for name, factor in factors.items():
        out[name] = (out[name] * factor).astype(out[name].dtype)
    return out
```

```python
from contextlib import ExitStack

import numpy as np

import concourse.bass as bass
from concourse import mybir

F32 = mybir.dt.float32
BF16 = mybir.dt.bfloat16
I32 = mybir.dt.int32
U32 = mybir.dt.uint32
U8 = mybir.dt.uint8
ALU = mybir.AluOpType
ACT = mybir.ActivationFunctionType
AX = mybir.AxisListType.X

P = 128
D = 1024
KD = D // P
NT = 5
TOK = NT * P
LAT = TOK - P
HA = 4
HB, GB, HD = 8, 2, 64
EPS = 1e-6
SCALE = HD ** -0.5
NEG = -1e30
PH, TOPK, NKEYS, NEXP = 8, 16, 128, 16384
LEVELS = 7
SLAB = 4096
NSLAB = 3
NGB = 4
HSLOTS = 2 * TOPK
CAND_ROWS = [(0, 1, 16), (1, 1, 8), (2, 1, 5), (3, 1, 4), (4, 1, 3), (5, 3, 2), (8, 8, 1)]
NCAND = sum(r * n for _, r, n in CAND_ROWS)
C_COND, C_BADA, C_N1, C_N2, C_LB, NCOLS = 0, 16, 64, 72, 80, 96
W_Q, W_I, W_FF, W_FB, W_AG, W_BQ, W_BKV, W_GA, W_GB = 0, 512, 1024, 1536, 2048, 2560, 3072, 3328, 4352
ADA_SEGS = [1, 0, 2, 3, 4, 5]
GATE_SEGS = (2, 5)

SLABS = ([("ada", s, half) for s in ADA_SEGS for half in range(2)]
         + [("win", c, n) for c, n in ((W_Q, 512), (W_FF, 512), (W_FB, 512), (W_I, 512), (W_AG, 512),
                                       (W_BQ, 512), (W_BKV, 256))]
         + [x for h in range(2) for x in (("win", W_GA + 512 * h, 512), ("win", W_GB + 512 * h, 512), ("wo", h, 0))]
         + [("wout", h, 0) for h in range(2)] + [("wpq", s, 0) for s in range(4)])
HEADS = [(t, h) for t in range(NT) for h in range(HB)]


def plan_groups():
    names = []
    for s in ADA_SEGS[:2]:
        names += [("ada", s, h) for h in range(2)]
    names += [("xT", t) for t in range(NT)]
    for s in ADA_SEGS[2:]:
        for h in range(2):
            names.append(("ada", s, h))
            if s in GATE_SEGS:
                names.append(("gate", s, h))
    names += [("winT", w, m) for w in (W_Q, W_FF, W_FB) for m in range(4)]
    names += [("win", w, t) for w in (W_I, W_AG, W_BQ, W_BKV) for t in range(NT)]
    for u in range(NT):
        names.append(("diag", u))
        names += [("lvl", u, l, d) for l in range(LEVELS) for d in range(2)]
        names += [("kT", u), ("dS", u), ("oA", u)]
    names += [("qkT", t) for t in range(NT)]
    for n in range(len(HEADS) + 2):
        if n < len(HEADS):
            names.append(("sc", n))
        if 0 <= n - 1 < len(HEADS):
            names.append(("pT", n - 1))
        if n >= 2 and (n - 2) % HB == 0:
            names.append(("oB", (n - 2) // HB))
    names += [("oT", t) for t in range(NT)]
    for half in range(2):
        names += [("gate_a", 4 * half + m) for m in range(4)] + [("gate_b", 4 * half + m) for m in range(4)]
        for m in range(4):
            names += [("ra", 4 * half + m), ("rb", 4 * half + m)]
    names += [("y", h, t) for h in range(2) for t in range(NT)]
    for t in range(NT):
        names += [("x2T", t), ("h2", t)]
    names += [("qp", 0)]
    for m in range(2 * PH):
        if m + 1 < 2 * PH:
            names.append(("qp", m + 1))
        names.append(("ss", m))
    place, turns, n, long = {}, [0] * 5, 0, 0
    for name in names:
        if name[0] in ("oA", "oB"):
            slot = 3 + long % 2
            long += 1
        else:
            slot = n % 3
            n += 1
        place[name] = (slot, turns[slot])
        turns[slot] += 1
    return names, place, turns


NAMES, PLACE, TURNS = plan_groups()


def build(nc, x_prompt, x_sample, cols, rows, normf_rows, brow, consts, masks, sel, w_ada, w_in, w_oa, w_ob, w_out,
          w_pq, keysT, uv, state, ckT, cv, y_prompt, y_sample, new_state, new_k, new_v):
    with ExitStack() as ctx:
        def sb(name, shape, dt=F32):
            return ctx.enter_context(nc.sbuf_tensor(name, shape, dt))

        def sem(name):
            return ctx.enter_context(nc.semaphore(name))

        X = sb("X", [P, NT, D])
        hT = sb("hT", [P, KD, TOK])
        GT = sb("GT", [P, 2, 2, D])
        RING = sb("RING", [P, NSLAB * SLAB])
        AB = sb("AB", [P, 15360])
        HG = sb("HG", [P, 5632])
        ST0 = sb("ST0", [P, 2, HA, P])
        CO = sb("CO", [P, NCOLS])
        RW = sb("RW", [P, 512 + HB])
        CT = sb("CT", [P, P + 640 + 2 * 4 * HD + NCAND])
        MK = sb("MK", [P, 15, P], U8)
        condT = sb("condT", [P, 2, KD])
        ADA = sb("ADA", [P, 4, 2, KD])
        AM = sb("AM", [P, 2, 2, KD])
        LB = sb("LB", [P, 2, 6, HA])
        st = sb("st", [P, 32])
        hst = sb("hst", [P, 16])
        ast = sb("ast", [P, NT * HB * 4 + 8])
        idxs = sb("idxs", [P, 2, TOPK], I32)
        gws = sb("gws", [P, 2, TOPK])
        apre = sb("apre", [P, 2, TOPK])
        agel = sb("agel", [P, 2, TOPK])
        wexp = sb("wexp", [P, 2, TOPK])
        ident = CT[:, 0:P]
        mbias = CT[:, P:P + 640]
        cosT = CT[:, P + 640:P + 640 + 256].rearrange("p (t d) -> p t d", t=4)
        sinT = CT[:, P + 896:P + 896 + 256].rearrange("p (t d) -> p t d", t=4)
        iota = CT[:, P + 1152:P + 1152 + NCAND]
        anorm, sink = RW[:, 0:512], RW[:, 512:512 + HB]

        def view(t, at, *dims):
            n = int(np.prod(dims))
            s = t[:, at:at + n]
            if len(dims) == 2:
                return s.rearrange("p (a b) -> p a b", a=dims[0])
            if len(dims) == 3:
                return s.rearrange("p (a b c) -> p a b c", a=dims[0], b=dims[1])
            return s

        BR = AB[0:2, 0:2 * D].rearrange("p (a b) -> p a b", a=2)
        GR = AB[0:2, 2048:2560]
        SEL = AB[0:2, 2560:2816].rearrange("p (a b) -> p a b", a=2)
        MK4 = view(AB, 5120, 15, P)
        QU = view(AB, 0, NT, 512)
        FU = [view(AB, 2560, NT, 512), view(AB, 5120, NT, 512)]
        IV = view(AB, 7680, NT, 512)
        OA = view(AB, 10240, NT, 512)
        BQ = view(AB, 12800, NT, 512)
        BKV = sb("BKV", [P, NT, 256])
        QT = view(AB, 0, NT, 512)
        KT = view(AB, 2560, NT, P)
        CKT, CV = view(HG, 0, 256), view(HG, 256, 2, P)
        SM, PR, PT = view(AB, 3200, 2, 640), view(AB, 4480, 2, 640), view(AB, 5760, 2, 640)
        OT = view(AB, 0, KD, TOK)
        MT = view(AB, 7680, KD, TOK)
        SA = view(HG, 0, 4, TOK)
        SBt = view(HG, 2560, 4, TOK)
        H2 = view(AB, 0, NT, D)
        SC = AB[:, 5120:5120 + NT * 2 * PH * P]
        KEYS = view(HG, 3072, 2 * PH, P)
        QP = view(HG, 0, 2, TOK)
        XN = view(HG, 0, 2, D)
        SQ = view(HG, 2048, D)
        HQ = [view(HG, 0, 512), view(HG, 512, 512)]
        HK = [view(HG, 1024, 512), view(HG, 1536, 512)]
        HT = [[view(HG, 2048, 256), view(HG, 2304, 128)], [view(HG, 2432, 256), view(HG, 2688, 128)]]
        HS = view(HG, 2816, 512)
        HKT = view(HG, 3328, 8, P)
        HST = view(HG, 4352, 2, 3, P)
        HSQ = view(HG, 5120, 512)
        RP1, RP2 = view(HG, 3072, 640), view(HG, 3712, 640)
        NST = [AB[:, 0:512], AB[:, 2560:3072]]
        hTf = hT[:].rearrange("p k t -> p (k t)")
        HC, NF = hTf[:, 0:D], hTf[:, D:2 * D]
        ZB = hTf[:, 2 * D:2 * D + 256].bitcast(BF16)
        GATH = [RING[:, i * 2 * D:(i + 1) * 2 * D] for i in range(NGB)]
        SCR = [RING[:, 8192 + i * D:8192 + (i + 1) * D] for i in range(2)]
        FIN = RING[:, 10240:10240 + 2 * D].rearrange("p (a b) -> p a b", a=2)
        DG = view(HG, 0, 2, P)
        RS, RS2 = view(HG, 256, 2 * NKEYS), view(HG, 512, 2 * NKEYS)
        RV, RI, RIF = view(HG, 768, 2, TOPK), HG[:, 800:832].bitcast(U32), HG[:, 832:864]
        RC, RC2, RCI = HG[:, 864:864 + NCAND], HG[:, 928:928 + NCAND], HG[:, 992:992 + NCAND]
        RT, RP, RPF = HG[:, 1056:1072], HG[:, 1072:1088].bitcast(U32), HG[:, 1088:1104]
        REQ = view(HG, 1104, TOPK, NCAND)
        RX = HG[:, 1936:1952]
        RM, RSUM, RR = HG[:, 1952:1953], HG[:, 1953:1954], HG[:, 1954:1955]
        RE = HG[:, 1956:1972]

        PS = [ctx.enter_context(nc.psum_tensor(f"ps{i}", [P, 1024], F32)) for i in range(3)]
        PL = ctx.enter_context(nc.psum_tensor("pl", [P, 1024], F32))

        def psum(slot):
            return PS[slot][:, :] if slot < 3 else PL[:, 512 * (slot - 3):512 * (slot - 2)]

        full = [sem(f"full{i}") for i in range(5)]
        free = [sem(f"free{i}") for i in range(5)]
        slab_in = [sem(f"slab_in{i}") for i in range(NSLAB)]
        x_in, small_in, misc_in = sem("x_in"), sem("small_in"), sem("misc_in")
        keys_in = sem("keys_in")
        act_step, dve_step, pool_step = sem("act_step"), sem("dve_step"), sem("pool_step")
        cond_ready, ada_ready, am_ready = sem("cond_ready"), sem("ada_ready"), sem("am_ready")
        ssq_ready, rms_ready, xn_ready, hT_ready = sem("ssq_ready"), sem("rms_ready"), sem("xn_ready"), sem("hT_ready")
        grow_ready, gate_ready = sem("grow_ready"), sem("gate_ready")
        lbx_ready, lbe_ready = sem("lbx_ready"), sem("lbe_ready")
        q_ready, sig_ready, f_ready = sem("q_ready"), sem("sig_ready"), sem("f_ready")
        iv_ready, ag_ready, oag_ready, bq_ready, bkv_ready = (sem("iv_ready"), sem("ag_ready"), sem("oag_ready"),
                                                             sem("bq_ready"), sem("bkv_ready"))
        rope_ready = sem("rope_ready")
        hg_ready = [sem("hgf_ready"), sem("hgb_ready")]
        hs_ready, kT_ready, st_ready = sem("hs_ready"), sem("kT_ready"), sem("st_ready")
        osq_ready, ossq_ready, orms_ready, oa_ready = sem("osq_ready"), sem("ossq_ready"), sem("orms_ready"), sem("oa_ready")
        nst_ready = sem("nst_ready")
        qkT_ready, sm_ready, p_ready, pT_ready, ob_ready = (sem("qkT_ready"), sem("sm_ready"), sem("p_ready"),
                                                            sem("pT_ready"), sem("ob_ready"))
        oT_ready, sig2_ready, m_ready, x1_ready = sem("oT_ready"), sem("sig2_ready"), sem("m_ready"), sem("x1_ready")
        h2T_ready, h2_ready = sem("h2T_ready"), sem("h2_ready")
        qp_ready, sc_ready = sem("qp_ready"), sem("sc_ready")
        kv_out, state_out, y_out = sem("kv_out"), sem("state_out"), [sem("y_out0"), sem("y_out1")]
        mk_ready = sem("mk_ready")
        nf_in, zb_ready, ctx_in = sem("nf_in"), sem("zb_ready"), sem("ctx_in")
        gath_in = [sem(f"gath_in{i}") for i in range(NGB)]
        go, waited = sem("go"), sem("waited")
        idx_ready, logit_ready, expo_ready, gw_ready = sem("idx_ready"), sem("logit_ready"), sem("expo_ready"), sem("gw_ready")
        route_step, u_done, gel_done, w_done, dg_done, v_done = (sem("route_step"), sem("u_done"), sem("gel_done"),
                                                                sem("w_done"), sem("dg_done"), sem("v_done"))
        acc_closed, acc_read, fss_ready, frt_ready, y_ready = (sem("acc_closed"), sem("acc_read"), sem("fss_ready"),
                                                              sem("frt_ready"), sem("y_ready"))

        def wait_full(eng, name):
            slot, turn = PLACE[name]
            eng.wait_ge(full[slot], turn + 1)
            return psum(slot)

        class Steps:

            def __init__(self, eng, s):
                self.eng, self.s, self.n = eng, s, 0

            def __call__(self, ins, *signals):
                self.n += 1
                ins.then_inc(self.s, 1)
                self.eng.wait_ge(self.s, self.n)
                for x in signals:
                    self.eng.sem_inc(x, 1)

        def freed(name):
            return free[PLACE[name][0]]

        def unit_block(u, b):
            return (0, b) if u == 0 else (b + 1, u - 1)

        def score_span(t):
            return (P, 2 * P) if t == 0 else (P if t == 1 else 0, 4 * P if t == NT - 1 else 5 * P)

        def half_update(d, l, mul, u):
            B = 1 << l
            T = FU[d][:, u, :] if l == 0 else HT[d][(l - 1) % 2][:, 0:512 >> l]
            T2 = T.rearrange("p (n a) -> p n a", a=2)
            q = HQ[d].rearrange("p (n a b) -> p n a b", a=2, b=B)
            k = HK[d].rearrange("p (n a b) -> p n a b", a=2, b=B)
            n = 256 // B
            lo, hi = T2[:, :, 0:1].to_broadcast([P, n, B]), T2[:, :, 1:2].to_broadcast([P, n, B])
            qh, kh = (1, 0) if d == 0 else (0, 1)
            yield mul(q[:, :, qh], q[:, :, qh], lo if d == 0 else hi)
            yield mul(k[:, :, kh], k[:, :, kh], hi if d == 0 else lo)
            yield mul(HT[d][l % 2][:, 0:n], T2[:, :, 0], T2[:, :, 1])

        block = ctx.enter_context(nc.Block())

        @block.sync
        def _(sp):
            sp.dma_start(CO[:], cols).then_inc(small_in, 16)
            sp.dma_start(CT[:], consts).then_inc(small_in, 16)
            sp.dma_start(SEL, sel).then_inc(small_in, 16)
            sp.dma_start(BR, brow).then_inc(small_in, 16)
            last_use = {}
            for n, (kind, a, b) in enumerate(SLABS):
                if kind == "ada":
                    last_use[n] = ("ada", a, b)
                elif kind == "win":
                    if a in (W_Q, W_FF, W_FB):
                        last_use[n] = ("winT", a, 3)
                    elif a >= W_GB:
                        last_use[n] = ("gate_b", 4 * ((a - W_GB) // 512) + 3)
                    elif a >= W_GA:
                        last_use[n] = ("gate_a", 4 * ((a - W_GA) // 512) + 3)
                    else:
                        last_use[n] = ("win", a, NT - 1)
                elif kind == "wo":
                    last_use[n] = ("rb", 4 * a + 3)
                elif kind == "wout":
                    last_use[n] = ("y", a, NT - 1)
                else:
                    last_use[n] = ("qp", 4 * a + 3)
            for n, (kind, a, b) in enumerate(SLABS):
                if n >= NSLAB:
                    wait_full(sp, last_use[n - NSLAB])
                at = RING[:, (n % NSLAB) * SLAB:(n % NSLAB + 1) * SLAB]
                s = slab_in[n % NSLAB]
                if kind == "ada":
                    sp.dma_start(at.rearrange("p (k n) -> p k n", k=KD),
                                 w_ada.rearrange("(k p) n -> p k n", p=P)[:, :, a * D + b * 512:a * D + b * 512 + 512]
                                 ).then_inc(s, 16)
                elif kind == "win":
                    sp.dma_start(at[:, 0:KD * b].rearrange("p (k n) -> p k n", k=KD),
                                 w_in.rearrange("(k p) n -> p k n", p=P)[:, :, a:a + b]).then_inc(s, 16)
                elif kind == "wo":
                    for i, w in enumerate((w_oa, w_ob)):
                        sp.dma_start(at[:, i * 2048:(i + 1) * 2048].rearrange("p (k n) -> p k n", k=4),
                                     w.rearrange("(k p) n -> p k n", p=P)[:, :, a * 512:(a + 1) * 512]).then_inc(s, 16)
                else:
                    w = w_out if kind == "wout" else w_pq
                    sp.dma_start(at.rearrange("p (k n) -> p k n", k=KD),
                                 w.rearrange("(k p) n -> p k n", p=P)[:, :, a * 512:(a + 1) * 512]).then_inc(s, 16)
                if n == 2:
                    sp.dma_start(X[:, 0, :], x_prompt).then_inc(x_in, 16)
                    sp.dma_start(X[:, 1:NT, :], x_sample.rearrange("(t p) d -> p t d", p=P)).then_inc(x_in, 16)
                    sp.dma_start(RW[:], rows).then_inc(misc_in, 16)
                    sp.dma_start(MK4, masks).then_inc(misc_in, 16)
                    sp.dma_start(ST0[:], state.rearrange("a h k v -> k a h v")).then_inc(misc_in, 16)
                if n == len(SLABS) - 4:
                    sp.wait_ge(m_ready, KD)
                    sp.dma_start(KEYS, keysT.rearrange("p (m n) -> p m n", m=2 * PH)).then_inc(keys_in, 16)
            wait_full(sp, ("qp", 2 * PH - 1))
            sp.dma_start(NF, normf_rows).then_inc(nf_in, 16)
            for t in range(NT):
                sp.wait_ge(y_ready, t + 1)
                dst = y_prompt if t == 0 else y_sample[(t - 1) * P:t * P, :]
                sp.dma_start(dst, FIN[:, t % 2, :]).then_inc(y_out[t % 2], 16)
            sp.wait_ge(y_out[0], 16 * 3)
            sp.wait_ge(y_out[1], 16 * 2)
            sp.wait_ge(kv_out, 32)
            sp.wait_ge(state_out, 32)

        slab_turn = {}
        for n, s_ in enumerate(SLABS):
            k = (n % NSLAB)
            slab_turn[s_] = (n % NSLAB, 16 * (sum(2 if SLABS[i][0] == "wo" else 1 for i in range(k, n + 1, NSLAB))))

        @block.tensor
        def _(pe):
            order = iter(NAMES)

            def start(name):
                assert next(order) == name, name
                slot, turn = PLACE[name]
                if turn:
                    pe.wait_ge(free[slot], turn)
                return psum(slot)

            def finish(name, ins):
                ins.then_inc(full[PLACE[name][0]], 1)

            def slab(*key):
                slot, count = slab_turn[key]
                pe.wait_ge(slab_in[slot], count)
                return RING[:, slot * SLAB:(slot + 1) * SLAB]

            def mm(out, l, r, s=True, e=True):
                return nc.tensor.matmul(out, l, r, start=s, stop=e)

            def tr(out, i):
                return nc.tensor.transpose(out, i, ident)

            def wide(ps, l, T, k, s, e):
                mm(ps[:, 0:LAT], l, T[:, k, P:TOK], s, e)
                return mm(ps[:, LAT:TOK], l, T[:, k, 0:P], s, e)

            def ada(s, half):
                w = slab("ada", s, half).rearrange("p (k n) -> p k n", k=KD)
                ps = start(("ada", s, half))
                if s in GATE_SEGS:
                    for k in range(KD):
                        last = mm(ps[0:2, 0:512], condT[:, :, k], w[:, k, :], k == 0, k == KD - 1)
                else:
                    for m in range(4):
                        for k in range(KD):
                            last = mm(ps[:, 2 * m:2 * m + 2], w[:, k, m * P:(m + 1) * P], condT[:, :, k],
                                      k == 0, k == KD - 1)
                finish(("ada", s, half), last)
                if s in GATE_SEGS:
                    n = 2 * GATE_SEGS.index(s) + half
                    pe.wait_ge(grow_ready, n + 1)
                    ps = start(("gate", s, half))
                    for c in range(2):
                        last = mm(ps[:, c * 512:(c + 1) * 512], SEL[:, c, :], GR)
                    finish(("gate", s, half), last)

            pe.wait_ge(small_in, 64)
            pe.wait_ge(cond_ready, 1)
            for s in ADA_SEGS[:2]:
                for half in range(2):
                    ada(s, half)

            def turn_x(name, t, n):
                pe.wait_ge(xn_ready, n + 1)
                ps = start((name, t))
                for k in range(KD):
                    last = tr(ps[:, k * P:(k + 1) * P], XN[:, t % 2, k * P:(k + 1) * P])
                finish((name, t), last)

            for t in range(NT):
                turn_x("xT", t, t)
            for s in ADA_SEGS[2:]:
                for half in range(2):
                    ada(s, half)
            pe.wait_ge(hT_ready, NT)
            for wc in (W_Q, W_FF, W_FB):
                w = slab("win", wc, 512).rearrange("p (k n) -> p k n", k=KD)
                for m in range(4):
                    ps = start(("winT", wc, m))
                    for k in range(KD):
                        last = wide(ps, w[:, k, m * P:(m + 1) * P], hT, k, k == 0, k == KD - 1)
                    finish(("winT", wc, m), last)
            for wc, n in ((W_I, 512), (W_AG, 512), (W_BQ, 512), (W_BKV, 256)):
                w = slab("win", wc, n)[:, 0:KD * n].rearrange("p (k n) -> p k n", k=KD)
                for t in range(NT):
                    ps = start(("win", wc, t))
                    for k in range(KD):
                        last = mm(ps[:, 0:n], hT[:, k, t * P:(t + 1) * P], w[:, k, :], k == 0, k == KD - 1)
                    finish(("win", wc, t), last)
            pe.wait_ge(iv_ready, NT)
            pe.wait_ge(misc_in, 48)
            for u in range(NT):
                bl = [slice(b * P, (b + 1) * P) for b in range(4)]
                for d in range(2):
                    pe.wait_ge(hg_ready[d], (LEVELS + 1) * u + 1)
                ps = start(("diag", u))
                for b in range(4):
                    mm(ps[:, bl[b]], HK[0][:, bl[b]], QU[:, u, bl[b]], True, False)
                    last = mm(ps[:, bl[b]], HK[1][:, bl[b]], QU[:, u, bl[b]], False, True)
                finish(("diag", u), last)
                for l in range(LEVELS):
                    for d in range(2):
                        pe.wait_ge(hg_ready[d], (LEVELS + 1) * u + l + 1)
                        ps = start(("lvl", u, l, d))
                        for b in range(4):
                            last = mm(ps[:, bl[b]], HK[d][:, bl[b]], HQ[d][:, bl[b]])
                        finish(("lvl", u, l, d), last)
                for d in range(2):
                    pe.wait_ge(hg_ready[d], (LEVELS + 1) * (u + 1))
                ps = start(("kT", u))
                for d in range(2):
                    for b in range(4):
                        last = tr(ps[:, (4 * d + b) * P:(4 * d + b + 1) * P], HK[d][:, bl[b]])
                finish(("kT", u), last)
                pe.wait_ge(kT_ready, u + 1)
                ps = start(("dS", u))
                for d in range(2):
                    for b in range(4):
                        t, h = unit_block(u, b)
                        last = mm(ps[:, (4 * d + b) * P:(4 * d + b + 1) * P], HKT[:, 4 * d + b, :],
                                  IV[:, t, h * P:(h + 1) * P])
                finish(("dS", u), last)
                pe.wait_ge(hs_ready, u + 1)
                pe.wait_ge(st_ready, u + 1)
                ps = start(("oA", u))
                for b in range(4):
                    t, h = unit_block(u, b)
                    last = mm(ps[:, bl[b]], HS[:, bl[b]], IV[:, t, h * P:(h + 1) * P], True, u == 0)
                    if u:
                        for d in range(2):
                            n = b if d == 0 else 3 - b
                            s0 = ST0[:, d, h, :] if n == 0 else HST[:, d, n - 1, :]
                            last = mm(ps[:, bl[b]], HQ[d][:, bl[b]], s0, False, d == 1)
                finish(("oA", u), last)
            pe.wait_ge(rope_ready, 4)
            pe.wait_ge(bkv_ready, NT)
            pe.wait_ge(bq_ready, NT)
            for t in range(NT):
                ps = start(("qkT", t))
                for j in range(4):
                    tr(ps[:, j * P:(j + 1) * P], BQ[:, t, j * P:(j + 1) * P])
                last = tr(ps[:, 512:640], BKV[:, t, 0:P])
                finish(("qkT", t), last)
            pe.wait_ge(qkT_ready, NT)
            pe.wait_ge(ctx_in, 32)

            def key_blocks(t):
                if t == 0:
                    return [(P, 0)]
                return [(c, k) for c, k in ((0, t - 1), (P, t), (2 * P, "c0"), (3 * P, "c1"), (4 * P, t + 1))
                        if not (k == 0 or k == NT)]

            def scores(n):
                t, h = HEADS[n]
                g, j = h // 4, h % 4
                r = slice(g * HD, (g + 1) * HD)
                ps = start(("sc", n))
                q = QT[r, t, j * P:(j + 1) * P]
                if t == 0:
                    last = mm(ps[:, P:2 * P], q, KT[r, 0, :])
                else:
                    if t > 1:
                        mm(ps[:, 0:P], q, KT[r, t - 1, :])
                    mm(ps[:, P:2 * P], q, KT[r, t, :])
                    last = mm(ps[:, 2 * P:4 * P], q, CKT[r, :])
                    if t < NT - 1:
                        last = mm(ps[:, 4 * P:5 * P], q, KT[r, t + 1, :])
                finish(("sc", n), last)

            def turn_p(n):
                t, h = HEADS[n]
                pe.wait_ge(p_ready, n + 1)
                ps = start(("pT", n))
                for c, _ in key_blocks(t):
                    last = tr(ps[:, c:c + P], PR[:, n % 2, c:c + P])
                finish(("pT", n), last)

            def values(n):
                t, h = HEADS[n]
                g = h // 4
                if h == 0:
                    start(("oB", t))
                pe.wait_ge(pT_ready, n + 1)
                ps = psum(PLACE[("oB", t)][0])
                kb = key_blocks(t)
                for i, (c, k) in enumerate(kb):
                    v = (CV[:, int(k[1]), g * HD:(g + 1) * HD] if isinstance(k, str)
                         else BKV[:, k, P + g * HD:P + (g + 1) * HD])
                    last = mm(ps[:, h * HD:(h + 1) * HD], PT[:, n % 2, c:c + P], v, i == 0, i == len(kb) - 1)
                if h == HB - 1:
                    finish(("oB", t), last)

            for n in range(len(HEADS) + 2):
                if n < len(HEADS):
                    scores(n)
                if 0 <= n - 1 < len(HEADS):
                    turn_p(n - 1)
                if n >= 2:
                    values(n - 2)
            pe.wait_ge(oa_ready, NT)
            for t in range(NT):
                pe.wait_ge(ob_ready, t + 1)
                ps = start(("oT", t))
                for k in range(4):
                    tr(ps[:, k * P:(k + 1) * P], OA[:, t, k * P:(k + 1) * P])
                for k in range(4):
                    last = tr(ps[:, (4 + k) * P:(5 + k) * P], BQ[:, t, k * P:(k + 1) * P])
                finish(("oT", t), last)
            for half in range(2):
                for wc, name in ((W_GA, "gate_a"), (W_GB, "gate_b")):
                    w = slab("win", wc + 512 * half, 512).rearrange("p (k n) -> p k n", k=KD)
                    for m in range(4):
                        ps = start((name, 4 * half + m))
                        for k in range(KD):
                            last = wide(ps, w[:, k, m * P:(m + 1) * P], hT, k, k == 0, k == KD - 1)
                        finish((name, 4 * half + m), last)
                w = slab("wo", half, 0).rearrange("p (a k n) -> p a k n", a=2, k=4)
                if half == 0:
                    pe.wait_ge(oT_ready, NT)
                for m in range(4):
                    for a, name in enumerate(("ra", "rb")):
                        ps = start((name, 4 * half + m))
                        for k in range(4):
                            last = wide(ps, w[:, a, k, m * P:(m + 1) * P], OT[:, 4 * a:4 * a + 4], k, k == 0, k == 3)
                        finish((name, 4 * half + m), last)
            pe.wait_ge(m_ready, KD)
            for half in range(2):
                w = slab("wout", half, 0).rearrange("p (k n) -> p k n", k=KD)
                for t in range(NT):
                    ps = start(("y", half, t))
                    for k in range(KD):
                        last = mm(ps[:, 0:512], MT[:, k, t * P:(t + 1) * P], w[:, k, :], k == 0, k == KD - 1)
                    finish(("y", half, t), last)
            for t in range(NT):
                turn_x("x2T", t, NT + t)
                pe.wait_ge(h2T_ready, t + 1)
                ps = start(("h2", t))
                for k in range(KD):
                    last = tr(ps[:, k * P:(k + 1) * P], hT[:, k, t * P:(t + 1) * P])
                finish(("h2", t), last)
            pe.wait_ge(keys_in, 16)

            def queries(m):
                w = slab("wpq", m // 4, 0).rearrange("p (k n) -> p k n", k=KD)
                ps = start(("qp", m))
                for k in range(KD):
                    last = wide(ps, w[:, k, (m % 4) * P:(m % 4 + 1) * P], hT, k, k == 0, k == KD - 1)
                finish(("qp", m), last)

            queries(0)
            for m in range(2 * PH):
                if m + 1 < 2 * PH:
                    queries(m + 1)
                pe.wait_ge(qp_ready, m + 1)
                ps = start(("ss", m))
                for i, t in enumerate((1, 2, 3, 4, 0)):
                    last = mm(ps[:, i * P:(i + 1) * P], QP[:, m % 2, i * P:(i + 1) * P], KEYS[:, m, :])
                finish(("ss", m), last)
            for s in range(3, 5):
                pe.wait_ge(free[s], TURNS[s])

            def pass_(base, p):
                for k in range(HSLOTS):
                    pe.wait_ge(dg_done, base + p * HSLOTS + k + 1)
                    for c in range(2):
                        last = nc.tensor.matmul(PL[:, c * 512:(c + 1) * 512], DG[:, k % 2, :],
                                                GATH[k % NGB][:, D + c * 512:D + (c + 1) * 512], start=False,
                                                stop=False, skip_group_check=True)
                    last.then_inc(v_done, 1)

            for t in range(NT):
                if t:
                    pe.wait_ge(acc_read, t)
                else:
                    pe.wait_ge(zb_ready, 1)
                for c in range(2):
                    nc.tensor.matmul(PL[:, c * 512:(c + 1) * 512], ZB[:, 0:P], ZB[:, :], start=True, stop=False,
                                     skip_group_check=True)
                with pe.Fori(0, 4) as p:
                    pass_(t * PH * TOPK, p)
                for c in range(2):
                    last = nc.tensor.matmul(PL[:, c * 512:(c + 1) * 512], ZB[:, 0:P], ZB[:, :], start=False,
                                            stop=True, skip_group_check=True)
                last.then_inc(acc_closed, 1)

        @block.scalar
        def _(act):
            step = Steps(act, act_step)
            A = nc.scalar.activation

            act.wait_ge(small_in, 64)
            step(A(condT[:].rearrange("p c k -> p (c k)"), CO[:, C_COND:C_COND + 16], ACT.Silu), cond_ready)
            act.wait_ge(lbx_ready, 1)
            step(A(LB[:, :, 2:4, :], LB[:, :, 0:2, :], ACT.Exp), lbe_ready)

            def norm_turn(n0, name, which, ready):
                for t in range(NT):
                    act.wait_ge(ssq_ready, n0 + t + 1)
                    step(A(st[:, 16 + t:17 + t], st[:, 8 + t:9 + t], ACT.Sqrt), rms_ready)
                act.wait_ge(am_ready, which + 1)
                for t in range(NT):
                    ps = wait_full(act, (name, t))
                    c = 0 if t == 0 else 1
                    shift = ADA[:, 1 + which, c, :]
                    for k in range(KD):
                        step(A(hT[:, k, t * P:(t + 1) * P], ps[:, k * P:(k + 1) * P], ACT.Identity,
                               scale=AM[:, which, c, k:k + 1], bias=shift[:, k:k + 1]))
                    act.sem_inc(freed((name, t)), 1)
                    act.sem_inc(ready, 1)
                    if which:
                        ps = wait_full(act, ("h2", t))
                        step(A(H2[:, t, :], ps, ACT.Copy), freed(("h2", t)), h2_ready)

            norm_turn(0, "xT", 0, hT_ready)
            for i, s in enumerate(GATE_SEGS):
                for half in range(2):
                    ps = wait_full(act, ("gate", s, half))
                    step(A(GT[:, i, :, half * 512:(half + 1) * 512], ps.rearrange("p (c n) -> p c n", c=2), ACT.Copy),
                         freed(("gate", s, half)), gate_ready)
            for wc, dst, fn, ready in ((W_Q, QU, ACT.Silu, q_ready), (W_FF, FU[0], ACT.Sigmoid, sig_ready),
                                       (W_FB, FU[1], ACT.Sigmoid, sig_ready)):
                if wc == W_FB:
                    act.wait_ge(mk_ready, 1)
                for m in range(4):
                    ps = wait_full(act, ("winT", wc, m))
                    step(A(dst[:, 1 + m, :], ps[:, 0:LAT], fn))
                    step(A(dst[:, 0, m * P:(m + 1) * P], ps[:, LAT:TOK], fn), freed(("winT", wc, m)), ready)
            for wc, n, dst, fn, ready in ((W_I, 512, IV, ACT.Copy, iv_ready), (W_AG, 512, OA, ACT.Silu, ag_ready),
                                          (W_BQ, 512, BQ, ACT.Copy, bq_ready), (W_BKV, 256, BKV, ACT.Copy, bkv_ready)):
                for t in range(NT):
                    ps = wait_full(act, ("win", wc, t))
                    o, i = dst[:, t, 0:n], ps[:, 0:n]
                    if wc == W_BQ:
                        o = o.rearrange("p (j g d) -> p j g d", j=4, g=GB)
                        i = i.rearrange("p (g j d) -> p j g d", j=4, g=GB)
                    step(A(o, i, fn), freed(("win", wc, t)), ready)
            for u in range(NT):
                ps = wait_full(act, ("kT", u))
                step(A(HKT.rearrange("p a b -> p (a b)"), ps, ACT.Copy), freed(("kT", u)), kT_ready)
                ps = wait_full(act, ("oA", u))
                step(A(HSQ, ps, ACT.Square), osq_ready)
                act.wait_ge(ossq_ready, u + 1)
                step(A(hst[:, 4:8], hst[:, 0:4], ACT.Sqrt), orms_ready)
            for t in range(NT):
                ps = wait_full(act, ("qkT", t))
                if t == 0:
                    act.wait_ge(oa_ready, NT)
                    act.wait_ge(state_out, 32)
                step(A(QT[:, t, :], ps[:, 0:512], ACT.Copy))
                step(A(KT[:, t, :], ps[:, 512:640], ACT.Copy), freed(("qkT", t)), qkT_ready)
            for n, (t, h) in enumerate(HEADS):
                lo, hi = score_span(t)
                act.wait_ge(sm_ready, n + 1)
                if n >= 2:
                    wait_full(act, ("pT", n - 2))
                step(A(PR[:, n % 2, lo:hi], SM[:, n % 2, lo:hi], ACT.Exp, bias=ast[:, 40 + n:41 + n], scale=SCALE,
                       accum_out=ast[:, 80 + n:81 + n]))
                step(A(ast[:, 120 + n:121 + n], sink[:, h:h + 1], ACT.Exp, bias=ast[:, 40 + n:41 + n]), p_ready)
            for t in range(NT):
                ps = wait_full(act, ("oT", t))
                if t == 0:
                    wait_full(act, ("oB", NT - 1))
                step(A(OT[:, :, t * P:(t + 1) * P], ps.rearrange("p (k n) -> p k n", k=KD), ACT.Copy),
                     freed(("oT", t)), oT_ready)
            for half in range(2):
                if half:
                    act.wait_ge(m_ready, 4)
                for name, dst in (("gate_a", SA), ("gate_b", SBt)):
                    for m in range(4):
                        ps = wait_full(act, (name, 4 * half + m))
                        step(A(dst[:, m, P:TOK], ps[:, 0:LAT], ACT.Sigmoid))
                        step(A(dst[:, m, 0:P], ps[:, LAT:TOK], ACT.Sigmoid), freed((name, 4 * half + m)), sig2_ready)
            norm_turn(NT, "x2T", 1, h2T_ready)
            for m in range(2 * PH):
                ps = wait_full(act, ("qp", m))
                if m >= 2:
                    wait_full(act, ("ss", m - 2))
                step(A(QP[:, m % 2, :], ps[:, 0:TOK], ACT.Copy), freed(("qp", m)), qp_ready)

            def expos(j):
                act.wait_ge(logit_ready, j + 1)
                A(RE, RT, ACT.Exp, bias=RM, accum_out=RSUM).then_inc(expo_ready, 1)

            def slots(base, p, h, ks):
                for k in ks:
                    n = base + p * HSLOTS + h * TOPK + k
                    act.wait_ge(u_done, n + 1 + 2)
                    A(agel[:, h, k:k + 1], apre[:, h, k:k + 1], ACT.Gelu).then_inc(gel_done, 1)
                    if k == 0:
                        act.wait_ge(gw_ready, base // TOPK + p * 2 + h + 1)
                    act.wait_ge(gel_done, n + 1)
                    A(wexp[:, h, k:k + 1], agel[:, h, k:k + 1], ACT.Copy, scale=gws[:, h, k:k + 1]).then_inc(w_done, 1)
                    act.wait_ge(w_done, n + 1)
                    act.wait_ge(v_done, n - 1 + NGB)
                    A(DG[:, k % 2, :], ident, ACT.Copy, scale=wexp[:, h, k:k + 1]).then_inc(dg_done, 1)

            expos(0)
            for t in range(NT):
                base = t * PH * TOPK

                def body(p, last):
                    j = t * PH + p * 2
                    slots(base, p, 0, range(3))
                    expos(j + 1)
                    slots(base, p, 0, range(3, TOPK))
                    slots(base, p, 1, range(3))
                    if not last:
                        expos(j + 2)
                    slots(base, p, 1, range(3, TOPK))

                with act.Fori(0, 4 if t < NT - 1 else 3) as p:
                    body(p, False)
                if t == NT - 1:
                    body(3, True)
                act.wait_ge(fss_ready, t + 1)
                A(st[:, 30:31], st[:, 29:30], ACT.Sqrt).then_inc(frt_ready, 1)

        @block.gpsimd
        def _(pool):
            step = Steps(pool, pool_step)
            pool.wait_ge(small_in, 64)
            pool.wait_ge(hT_ready, NT)
            for t in range(1, NT):
                pool.wait_ge(bq_ready, t + 1)
                pool.wait_ge(bkv_ready, t + 1)
                for src, n, at in ((BQ[:, t, :], HB, 0), (BKV[:, t, 0:P], GB, 512)):
                    r1 = RP1[:, at:at + n * HD].rearrange("p (h d) -> p h d", h=n)
                    r2 = RP2[:, at:at + n * HD].rearrange("p (h f d) -> p h f d", h=n, f=2)
                    s3 = src.rearrange("p (h d) -> p h d", h=n)
                    s4 = src.rearrange("p (h f d) -> p h f d", h=n, f=2)
                    step(nc.gpsimd.tensor_tensor(r1, s3, cosT[:, t - 1, :].unsqueeze(1).to_broadcast([P, n, HD]),
                                                 ALU.mult))
                    sn = sinT[:, t - 1, :].rearrange("p (f d) -> p f d", f=2)
                    for a in range(2):
                        step(nc.gpsimd.tensor_tensor(
                            r2[:, :, :, a * 16:(a + 1) * 16], s4[:, :, :, (1 - a) * 16:(2 - a) * 16],
                            sn[:, :, a * 16:(a + 1) * 16].unsqueeze(1).to_broadcast([P, n, 2, 16]), ALU.mult))
                    step(nc.gpsimd.tensor_tensor(src, RP1[:, at:at + n * HD], RP2[:, at:at + n * HD], ALU.add))
                pool.sem_inc(rope_ready, 1)
            pool.wait_ge(bkv_ready, 1)
            pool.dma_start(new_k, BKV[:, 0, 0:P]).then_inc(kv_out, 16)
            pool.dma_start(new_v, BKV[:, 0, P:2 * P]).then_inc(kv_out, 16)
            pool.wait_ge(f_ready, 2)
            pool.wait_ge(q_ready, 4)

            def mul(o, a, b):
                return nc.gpsimd.tensor_tensor(o, a, b, ALU.mult)

            for u in range(NT):
                if u:
                    wait_full(pool, ("oA", u - 1))
                step(nc.gpsimd.tensor_scalar(HK[1], FU[1][:, u, :], -1.0, 1.0, ALU.mult, ALU.add))
                step(mul(HQ[1], QU[:, u, :], FU[1][:, u, :]), hg_ready[1])
                for l in range(LEVELS):
                    wait_full(pool, ("lvl", u, l, 1))
                    for ins in half_update(1, l, mul, u):
                        step(ins)
                    pool.sem_inc(hg_ready[1], 1)
                if u:
                    continue
                for d in range(2):
                    pool.wait_ge(nst_ready, 1)
                    pool.dma_start(new_state[d].rearrange("h k v -> k h v"),
                                   NST[d].rearrange("p (h v) -> p h v", h=HA)).then_inc(state_out, 16)
            pool.wait_ge(oa_ready, NT)
            pool.dma_start(CKT, ckT).then_inc(ctx_in, 16)
            pool.dma_start(CV, cv.rearrange("(b p) n -> p b n", p=P)).then_inc(ctx_in, 16)

            def gathers(base, p):
                for h in range(2):
                    j = base // TOPK + p * 2 + h
                    pool.wait_ge(idx_ready, j + 1)
                    pool.sem_inc(go, 1)
                    for k in range(TOPK):
                        pool.wait_ge(v_done, base + p * HSLOTS + h * TOPK + k + 1)
                        pool.sem_inc(go, 1)
                        nc.gpsimd.indirect_dma_start(
                            out=GATH[k % NGB], out_offset=None, in_=uv,
                            in_offset=bass.IndirectOffsetOnAxis(ap=idxs[:, h, k:k + 1], axis=0)
                        ).then_inc(gath_in[k % NGB], 16)

            wait_full(pool, ("qp", 2 * PH - 1))
            pool.memset(ZB, 0.0).then_inc(zb_ready, 1)
            pool.sem_inc(v_done, NGB)
            for t in range(NT):
                with pool.Fori(0, 4) as p:
                    gathers(t * PH * TOPK, p)

        @block.vector
        def _(dve):
            step = Steps(dve, dve_step)
            V = nc.vector

            dve.wait_ge(small_in, 64)
            lg = CO[:, C_LB:C_LB + 16].rearrange("p (d l h) -> p d l h", d=2, l=2)
            step(V.tensor_tensor(LB[:, :, 4, :], lg[:, :, 0], lg[:, :, 1], ALU.max))
            for l in range(2):
                last = V.tensor_tensor(LB[:, :, l, :], lg[:, :, l], LB[:, :, 4, :], ALU.subtract)
                step(last)
            dve.sem_inc(lbx_ready, 1)
            dve.wait_ge(lbe_ready, 1)
            step(V.tensor_tensor(LB[:, :, 4, :], LB[:, :, 2, :], LB[:, :, 3, :], ALU.add))
            step(V.reciprocal(LB[:, :, 5, :], LB[:, :, 4, :]))
            step(V.tensor_tensor(LB[:, :, 0, :], LB[:, :, 2, :], LB[:, :, 5, :], ALU.mult))
            step(V.tensor_scalar(LB[:, :, 1, :], LB[:, :, 0, :], -1.0, 1.0, ALU.mult, ALU.add))

            def ssq(n, t):
                step(V.tensor_tensor_reduce(out=SQ, in0=X[:, t, :], in1=X[:, t, :], scale=1.0, scalar=0.0,
                                            op0=ALU.mult, op1=ALU.add, accum_out=st[:, t:t + 1]))
                step(V.tensor_scalar(st[:, 8 + t:9 + t], st[:, t:t + 1], 1.0 / D, EPS, ALU.mult, ALU.add), ssq_ready)

            def normed(n0, name):
                for t in range(NT):
                    dve.wait_ge(rms_ready, n0 + t + 1)
                    step(V.reciprocal(st[:, 24:25], st[:, 16 + t:17 + t]))
                    if t >= 2:
                        wait_full(dve, (name, t - 2))
                    step(V.tensor_scalar(XN[:, t % 2, :], X[:, t, :], st[:, 24:25], None, ALU.mult), xn_ready)

            dve.wait_ge(x_in, 32)
            for t in range(NT):
                ssq(t, t)

            dve.wait_ge(misc_in, 48)
            step(V.tensor_copy(MK[:], MK4), mk_ready)

            def ada_cols(s):
                which = {1: 0, 0: 1, 3: 2, 4: 3}[s]
                for half in range(2):
                    ps = wait_full(dve, ("ada", s, half))
                    b = CO[:, C_BADA + 8 * s + 4 * half:C_BADA + 8 * s + 4 * half + 4]
                    step(V.tensor_tensor(ADA[:, which, :, 4 * half:4 * half + 4],
                                         ps[:, 0:8].rearrange("p (m c) -> p c m", c=2),
                                         b.unsqueeze(1).to_broadcast([P, 2, 4]), ALU.add), freed(("ada", s, half)))

            def scaled(which, col, at):
                for c in range(2):
                    step(V.scalar_tensor_tensor(AM[:, which, c, :], ADA[:, at, c, :], 1.0, CO[:, col:col + 8],
                                                ALU.add, ALU.mult))
                dve.sem_inc(am_ready, 1)

            ada_cols(1)
            ada_cols(0)
            scaled(0, C_N1, 0)
            normed(0, "xT")
            for s in ADA_SEGS[2:]:
                if s in GATE_SEGS:
                    i = GATE_SEGS.index(s)
                    for half in range(2):
                        ps = wait_full(dve, ("ada", s, half))
                        n = 2 * i + half
                        if n:
                            wait_full(dve, ("gate", GATE_SEGS[(n - 1) // 2], (n - 1) % 2))
                        step(V.tensor_tensor(GR, ps[0:2, 0:512], BR[:, i, half * 512:(half + 1) * 512], ALU.add),
                             freed(("ada", s, half)), grow_ready)
                else:
                    ada_cols(s)
            scaled(1, C_N2, 3)
            for d in range(2):
                dve.wait_ge(sig_ready, 4 * d + 4)
                for h in range(HA):
                    a, b = LB[:, d, 1, h:h + 1], LB[:, d, 0, h:h + 1]
                    for part in (FU[d][:, 1 + h, :], FU[d][:, 0, h * P:(h + 1) * P]):
                        step(V.tensor_scalar(part, part, a, b, ALU.mult, ALU.add))
                dve.sem_inc(f_ready, 1)
            dve.wait_ge(misc_in, 48)
            dve.wait_ge(q_ready, 4)
            for t in range(NT):
                dve.wait_ge(ag_ready, t + 1)
                step(V.tensor_tensor(OA[:, t, :], OA[:, t, :], anorm, ALU.mult))

            def mul(o, a, b):
                return V.tensor_tensor(o, a, b, ALU.mult)

            dve.wait_ge(rope_ready, 4)
            HS3 = HS.rearrange("p (b n) -> p b n", b=4)

            def take(name, m):
                ps = wait_full(dve, name)
                step(V.copy_predicated(HS3, MK[:, m, :].unsqueeze(1).to_broadcast([P, 4, P]),
                                       ps[:, 0:512].rearrange("p (b n) -> p b n", b=4)), freed(name))

            for u in range(NT):
                if u:
                    wait_full(dve, ("oA", u - 1))
                step(V.tensor_scalar(HK[0], FU[0][:, u, :], -1.0, 1.0, ALU.mult, ALU.add))
                step(mul(HQ[0], QU[:, u, :], FU[0][:, u, :]), hg_ready[0])
                take(("diag", u), 14)
                for l in range(LEVELS):
                    take(("lvl", u, l, 0), l)
                    for ins in half_update(0, l, mul, u):
                        step(ins)
                    dve.sem_inc(hg_ready[0], 1)
                    take(("lvl", u, l, 1), 7 + l)
                dve.sem_inc(hs_ready, 1)
                dve.wait_ge(hg_ready[1], (LEVELS + 1) * (u + 1))
                ps = wait_full(dve, ("dS", u))
                if u == 0:
                    step(V.tensor_copy(NST[0], ps[:, 0:512]))
                    step(V.tensor_copy(NST[1], ps[:, 512:1024]), freed(("dS", u)), nst_ready, st_ready)
                else:
                    for d in range(2):
                        tot = HT[d][(LEVELS - 1) % 2]
                        for n in range(3):
                            b = n if d == 0 else 3 - n
                            s0 = ST0[:, d, u - 1, :] if n == 0 else HST[:, d, n - 1, :]
                            step(V.scalar_tensor_tensor(HST[:, d, n, :], s0, tot[:, b:b + 1],
                                                        ps[:, (4 * d + b) * P:(4 * d + b + 1) * P], ALU.mult, ALU.add))
                    dve.sem_inc(freed(("dS", u)), 1)
                    dve.sem_inc(st_ready, 1)
                ps = psum(PLACE[("oA", u)][0])
                dve.wait_ge(osq_ready, u + 1)
                step(V.tensor_reduce(hst[:, 8:12], HSQ.rearrange("p (b n) -> p b n", b=4), AX, ALU.add))
                step(V.tensor_scalar(hst[:, 0:4], hst[:, 8:12], 1.0 / P, EPS, ALU.mult, ALU.add), ossq_ready)
                dve.wait_ge(orms_ready, u + 1)
                step(V.reciprocal(hst[:, 12:16], hst[:, 4:8]))
                for b in range(4):
                    t, h = unit_block(u, b)
                    o = OA[:, t, h * P:(h + 1) * P]
                    step(V.scalar_tensor_tensor(o, ps[:, b * P:(b + 1) * P], hst[:, 12 + b:13 + b], o,
                                                ALU.mult, ALU.mult))
                dve.sem_inc(freed(("oA", u)), 1)
                dve.sem_inc(oa_ready, 1)
            step(V.tensor_scalar(ast[:, 160:168], sink, -1.0, None, ALU.mult))

            def row_max(n):
                t, h = HEADS[n]
                lo, hi = score_span(t)
                ps = wait_full(dve, ("sc", n))
                if n >= 2:
                    dve.wait_ge(p_ready, n - 1)
                step(V.tensor_tensor_reduce(out=SM[:, n % 2, lo:hi], in0=ps[:, lo:hi], in1=mbias[:, lo:hi], scale=1.0,
                                            scalar=NEG, op0=ALU.add, op1=ALU.max, accum_out=ast[:, n:n + 1]),
                     freed(("sc", n)))
                step(V.tensor_scalar(ast[:, 40 + n:41 + n], ast[:, n:n + 1], -SCALE, ast[:, 160 + h:161 + h],
                                     ALU.mult, ALU.min), sm_ready)

            def copy_pT(n):
                t, h = HEADS[n]
                lo, hi = score_span(t)
                ps = wait_full(dve, ("pT", n))
                step(V.tensor_copy(PT[:, n % 2, lo:hi], ps[:, lo:hi]), freed(("pT", n)), pT_ready)

            def out_b(t):
                dve.wait_ge(p_ready, HB * (t + 1))
                s = slice(80 + HB * t, 88 + HB * t)
                step(V.tensor_tensor(ast[:, s], ast[:, s], ast[:, 120 + HB * t:128 + HB * t], ALU.add))
                step(V.reciprocal(ast[:, s], ast[:, s]))
                ps = wait_full(dve, ("oB", t))
                step(V.tensor_tensor(BQ[:, t, :].rearrange("p (h d) -> p h d", h=HB),
                                     ps.rearrange("p (h d) -> p h d", h=HB),
                                     ast[:, s].unsqueeze(2).to_broadcast([P, HB, HD]), ALU.mult),
                     freed(("oB", t)), ob_ready)

            for n in range(len(HEADS) + 2):
                if n < len(HEADS):
                    if n == 0:
                        dve.wait_ge(qkT_ready, NT)
                    row_max(n)
                if 0 <= n - 1 < len(HEADS):
                    copy_pT(n - 1)
                if n >= 2 and (n - 2) % HB == HB - 1:
                    out_b((n - 2) // HB)
            for half in range(2):
                for m in range(4):
                    n = 4 * half + m
                    for i, (name, dst) in enumerate((("ra", SA), ("rb", SBt))):
                        dve.wait_ge(sig2_ready, 8 * half + 4 * i + m + 1)
                        ps = wait_full(dve, (name, n))
                        step(V.tensor_tensor(dst[:, m, P:TOK], ps[:, 0:LAT], dst[:, m, P:TOK], ALU.mult))
                        step(V.tensor_tensor(dst[:, m, 0:P], ps[:, LAT:TOK], dst[:, m, 0:P], ALU.mult),
                             freed((name, n)))
                    step(V.tensor_tensor(MT[:, n, :], SA[:, m, :], SBt[:, m, :], ALU.add), m_ready)
            dve.wait_ge(gate_ready, 4)
            for half in range(2):
                for t in range(NT):
                    c = 0 if t == 0 else 1
                    ps = wait_full(dve, ("y", half, t))
                    cs = slice(half * 512, (half + 1) * 512)
                    step(V.tensor_tensor(SQ[:, 0:512], ps[:, 0:512], GT[:, 0, c, cs], ALU.mult), freed(("y", half, t)))
                    step(V.tensor_tensor(X[:, t, cs], X[:, t, cs], SQ[:, 0:512], ALU.add))
                    if half:
                        ssq(NT + t, t)
            XN2 = XN
            for t in range(NT):
                dve.wait_ge(rms_ready, NT + t + 1)
                step(V.reciprocal(st[:, 24:25], st[:, 16 + t:17 + t]))
                if t >= 2:
                    wait_full(dve, ("x2T", t - 2))
                step(V.tensor_scalar(XN[:, t % 2, :], X[:, t, :], st[:, 24:25], None, ALU.mult), xn_ready)
            for m in range(2 * PH):
                ps = wait_full(dve, ("ss", m))
                s3 = SC.rearrange("p (t m n) -> p t m n", t=NT, m=2 * PH)
                step(V.tensor_copy(s3[:, 1:NT, m, :], ps[:, 0:LAT].rearrange("p (t n) -> p t n", t=NT - 1)))
                step(V.tensor_copy(s3[:, 0, m, :], ps[:, LAT:TOK]), freed(("ss", m)), sc_ready)

            def route(j, par, count):
                n = [0]

                def r(ins):
                    n[0] += 1
                    ins.then_inc(route_step, 1)
                    dve.wait_ge(route_step, count(n[0]))

                def top16(v, ix, src, tmp):
                    for f in (lambda: V.max(v[:, 0:8], src), lambda: V.max_index(ix[:, 0:8], v[:, 0:8], src),
                              lambda: V.match_replace(tmp, v[:, 0:8], src, -3e38),
                              lambda: V.max(v[:, 8:16], tmp), lambda: V.max_index(ix[:, 8:16], v[:, 8:16], tmp)):
                        dve.sem_inc(waited, 1)
                        r(f())

                r(V.tensor_copy(RS, SC[:, bass.ds(j * 2 * NKEYS, 2 * NKEYS)]))
                for a in range(2):
                    top16(RV[:, a, :], RI[:, a * TOPK:(a + 1) * TOPK], RS[:, a * NKEYS:(a + 1) * NKEYS],
                          RS2[:, a * NKEYS:(a + 1) * NKEYS])
                r(V.tensor_copy(RIF, RI))
                r(V.tensor_scalar(RIF[:, 0:TOPK], RIF[:, 0:TOPK], float(NKEYS), None, ALU.mult))
                at = 0
                for i, rows_, w in CAND_ROWS:
                    for dst, s1, s2 in ((RC, RV[:, 0, :], RV[:, 1, :]), (RCI, RIF[:, 0:TOPK], RIF[:, TOPK:2 * TOPK])):
                        r(V.tensor_tensor(dst[:, at:at + rows_ * w].rearrange("p (a b) -> p a b", a=rows_),
                                          s1[:, i:i + rows_].unsqueeze(2).to_broadcast([P, rows_, w]),
                                          s2[:, 0:w].unsqueeze(1).to_broadcast([P, rows_, w]), ALU.add))
                    at += rows_ * w
                top16(RT, RP, RC, RC2)
                r(V.tensor_scalar(RM, RT[:, 0:1], -1.0, None, ALU.mult))
                dve.sem_inc(logit_ready, 1)
                r(V.tensor_copy(RPF, RP))
                r(V.tensor_tensor(REQ, iota.unsqueeze(1).to_broadcast([P, TOPK, NCAND]),
                                  RPF.unsqueeze(2).to_broadcast([P, TOPK, NCAND]), ALU.is_equal))
                r(V.tensor_tensor(REQ, REQ, RCI.unsqueeze(1).to_broadcast([P, TOPK, NCAND]), ALU.mult))
                r(V.tensor_reduce(RX, REQ, AX, ALU.add))
                r(V.tensor_copy(idxs[:, par, :], RX))
                dve.sem_inc(idx_ready, 1)
                dve.wait_ge(expo_ready, j + 1)
                r(V.reciprocal(RR, RSUM))
                if not (isinstance(j, int) and j == 0):
                    dve.wait_ge(v_done, (j - 1) * TOPK + NGB)
                r(V.tensor_scalar(gws[:, par, :], RE, RR, None, ALU.mult))
                dve.sem_inc(gw_ready, 1)
                return n[0]

            def dots(base, p, h, ks):
                for k in ks:
                    n = base + p * HSLOTS + h * TOPK + k
                    per = HSLOTS // NGB
                    dve.wait_ge(gath_in[k % NGB],
                                16 * (base // NGB) + p * (16 * per) + 16 * ((h * TOPK + k) // NGB + 1))
                    dve.wait_ge(u_done, n - 1 + 2)
                    V.tensor_tensor_reduce(out=SCR[k % 2], in0=GATH[k % NGB][:, 0:D], in1=HC, scale=1.0, scalar=0.0,
                                           op0=ALU.mult, op1=ALU.add, accum_out=apre[:, h, k:k + 1]).then_inc(u_done, 1)

            wait_full(dve, ("ss", 2 * PH - 1))
            dve.wait_ge(h2_ready, NT)
            dve.sem_inc(u_done, 2)
            dve.wait_ge(nf_in, 16)
            RSTEPS = route(0, 0, lambda n: n)
            for t in range(NT):
                base = t * PH * TOPK
                step(V.tensor_copy(HC, H2[:, t, :]))

                def pass_(p, last):
                    for h in range(2):
                        dots(base, p, h, range(3))
                        if not (last and h):
                            j = t * PH + p * 2 + h + 1
                            route(j, 1 - h, lambda n: j * RSTEPS + n)
                        dots(base, p, h, range(3, TOPK))

                with dve.Fori(0, 4 if t < NT - 1 else 3) as p:
                    pass_(p, False)
                if t == NT - 1:
                    pass_(3, True)
                dve.wait_ge(u_done, base + PH * TOPK + 2)
                dve.wait_ge(acc_closed, t + 1)
                c = 0 if t == 0 else 1
                step(V.tensor_tensor(SCR[0], PL[:, :], GT[:, 1, c, :], ALU.mult), acc_read)
                step(V.tensor_tensor(X[:, t, :], X[:, t, :], SCR[0], ALU.add))
                step(V.tensor_tensor_reduce(out=SCR[1], in0=X[:, t, :], in1=X[:, t, :], scale=1.0, scalar=0.0,
                                            op0=ALU.mult, op1=ALU.add, accum_out=st[:, 28:29]))
                step(V.tensor_scalar(st[:, 29:30], st[:, 28:29], 1.0 / D, EPS, ALU.mult, ALU.add), fss_ready)
                dve.wait_ge(frt_ready, t + 1)
                step(V.reciprocal(st[:, 31:32], st[:, 30:31]))
                if t >= 2:
                    dve.wait_ge(y_out[t % 2], 16 * (t // 2))
                step(V.scalar_tensor_tensor(FIN[:, t % 2, :], X[:, t, :], st[:, 31:32], NF, ALU.mult, ALU.mult),
                     y_ready)


def shape_constants():
    f = np.float32
    i = np.arange(P)
    ident = np.eye(P, dtype=f)
    left = np.where(i[None, :] >= i[:, None], 0.0, NEG).astype(f)
    right = np.where(i[None, :] <= i[:, None], 0.0, NEG).astype(f)
    mbias = np.concatenate([left, np.zeros((P, 3 * P), f), right], axis=1)
    pos = np.arange(LAT)
    nf = HD // 4
    inv = f(10000.0) ** (-np.arange(nf, dtype=f) / f(nf))
    ang = [(a.astype(f)[:, None] * inv[None, :]).astype(f) for a in (pos // 64, pos % 64)]
    cos = np.concatenate([np.cos(a) for a in ang for _ in range(2)], axis=1).astype(f)
    sin = np.concatenate([x for a in ang for x in (-np.sin(a), np.sin(a))], axis=1).astype(f)
    lay = lambda a: a.reshape(NT - 1, P, HD).transpose(1, 0, 2).reshape(P, -1)
    iota = np.broadcast_to(np.arange(NCAND, dtype=f), (P, NCAND))
    consts = np.concatenate([ident, mbias, lay(cos), lay(sin), iota], axis=1)
    masks = np.zeros((P, 15, P), f)
    s, t = i[:, None], i[None, :]
    for l in range(LEVELS):
        same = (s >> (l + 1)) == (t >> (l + 1))
        masks[:, l] = same & ((s >> l) % 2 == 0) & ((t >> l) % 2 == 1)
        masks[:, 7 + l] = same & ((s >> l) % 2 == 1) & ((t >> l) % 2 == 0)
    masks[:, 14] = s == t
    sel = np.zeros((2, 2, P), f)
    sel[0, 0] = 1
    sel[1, 1] = 1
    return consts, masks, sel


_OUTS = [(1, P, D), (1, LAT, D), (1, 1, 2, HA, P, P), (1, 1, P, GB, HD), (1, 1, P, GB, HD)]


def kernel(x_prompt, x_sample, state_hgrn, cache_k, cache_v, c, c_ctx, w_ada, b_ada, norm1, norm2, w_in, lb_logits,
           a_norm, b_sink, w_oa, w_ob, w_out, p_wq, p_keys, p_u, p_v, norm_f):
    import concourse.bacc as _bacc
    from concourse import mybir as _mybir
    from concourse.bass_utils import run_bass_kernel_spmd as _run

    a = np.asarray
    spread = lambda v: np.broadcast_to(a(v).reshape(1, -1), (P, a(v).size))
    consts, masks, sel = shape_constants()
    b = a(b_ada)[0].reshape(6, D)
    arrays = {
        "x_prompt": a(x_prompt)[0], "x_sample": a(x_sample)[0],
        "cols": np.concatenate([a(c_ctx).reshape(-1, P), a(c).reshape(-1, P), a(b_ada).reshape(-1, P),
                                a(norm1).reshape(-1, P), a(norm2).reshape(-1, P), a(lb_logits).reshape(-1, P)]).T,
        "rows": np.concatenate([spread(a_norm), spread(b_sink)], axis=1),
        "normf_rows": spread(norm_f),
        "brow": np.stack([b[[2, 5]], b[[2, 5]]]),
        "consts": consts, "masks": masks, "sel": sel,
        "w_ada": a(w_ada)[0], "w_in": a(w_in)[0], "w_oa": a(w_oa)[0], "w_ob": a(w_ob)[0], "w_out": a(w_out)[0],
        "w_pq": a(p_wq)[0],
        "keysT": a(p_keys)[0].reshape(2 * PH, NKEYS, P).transpose(2, 0, 1).reshape(P, -1),
        "uv": np.concatenate([a(p_u)[0], a(p_v)[0]], axis=1),
        "state": a(state_hgrn)[0, 0],
        "ckT": a(cache_k)[0, 0].reshape(256, GB * HD).T,
        "cv": a(cache_v)[0, 0].reshape(256, GB * HD),
    }
    arrays = {k: np.ascontiguousarray(v) for k, v in arrays.items()}
    nc = _bacc.Bacc("TRN2", target_bir_lowering=False, num_devices=1)
    args = [nc.dram_tensor(f"in_{k}", v.shape, _mybir.dt.from_np(v.dtype), kind="ExternalInput").ap()
            for k, v in arrays.items()]
    outs = [nc.dram_tensor(f"out_{i}", s, _mybir.dt.float32, kind="ExternalOutput").ap() for i, s in enumerate(_OUTS)]
    build(nc, *args, outs[0][0], outs[1][0], outs[2][0, 0], outs[3][0, 0].rearrange("s g d -> s (g d)"),
          outs[4][0, 0].rearrange("s g d -> s (g d)"))
    r = _run(nc, [{f"in_{k}": v for k, v in arrays.items()}], core_ids=[0])
    return tuple(r.results[0][f"out_{i}"] for i in range(len(_OUTS)))
```

```python
from contextlib import ExitStack

import numpy as np

import concourse.bass as bass
from concourse import mybir

F32 = mybir.dt.float32
BF16 = mybir.dt.bfloat16
I32 = mybir.dt.int32
U32 = mybir.dt.uint32
U8 = mybir.dt.uint8
ALU = mybir.AluOpType
ACT = mybir.ActivationFunctionType
AX = mybir.AxisListType.X

P = 128
D = 1024
KD = D // P
NT = 5
TOK = NT * P
LAT = TOK - P
HA = 4
HB, GB, HD = 8, 2, 64
EPS = 1e-6
SCALE = HD ** -0.5
NEG = -1e30
PH, TOPK, NKEYS = 8, 16, 128
TSLOT = PH * TOPK
LEVELS = 7
SLAB = 2048
SC_W = 256
SLOTW = SLAB + 2 * NKEYS
NSLAB = 3
NGA, NGB = 4, 8
HSLOTS = 2 * TOPK
CAND_ROWS = [(0, 1, 16), (1, 1, 8), (2, 1, 5), (3, 1, 4), (4, 1, 3), (5, 3, 2), (8, 8, 1)]
NCAND = sum(r * n for _, r, n in CAND_ROWS)
C_COND, C_BADA, C_N1, C_N2, C_LB, NCOLS = 0, 16, 64, 72, 80, 96
W_Q, W_I, W_FF, W_FB, W_AG, W_BQ, W_BKV, W_GA, W_GB = 0, 512, 1024, 1536, 2048, 2560, 3072, 3328, 4352
ADA_SEGS = [1, 0, 2, 3, 4, 5]
NADA = 4 * len(ADA_SEGS)
GATE_SEGS = (2, 5)
BATCHES = [(0,), (1,), (2, 3, 4)]
WIN_T = (W_Q, W_FF, W_FB)
WIN = [(W_BQ, 0), (W_BQ, 1), (W_BKV, 0), (W_I, 0), (W_I, 1), (W_AG, 0), (W_AG, 1)]
HEADS = [(t, h) for t in range(NT) for h in range(HB)]
ROUTE_AT = {1: 0, 2: 1, 3: 2, 4: 3, 5: 4, 7: 5}
EXPO_AT = 5
SHARE = {"winT": 4.0, "win": 2.0, "diag": 1.3, "lvl": 1.3, "kT": 1.3, "dS": 1.3, "oA": 1.3,
         "qkT": 1.0, "sc": 1.0, "pT": 1.0, "oB": 1.0, "oT": 0.6, "gate_a": 1.0, "gate_b": 1.0, "ra": 0.5, "rb": 0.5,
         "y": 0.67, "x2T": 0.6, "h2": 0.6, "qp": 1.0, "ss": 0.2}
POOL_LEAD = 3

SLABS = ([("ada", n) for n in range(NADA)]
         + [("winT", w, m) for w in WIN_T for m in range(2)]
         + [("win", w, a) for w, a in WIN])
for _b in range(len(BATCHES)):
    for _q in range(4):
        SLABS += [("gate_a", _b, _q), ("gate_b", _b, _q), ("wo", _b, _q)]
    SLABS += [("wout", _b, _q) for _q in range(4)] + [("wpq", _b, _q) for _q in range(8)]
    if _b == 0:
        SLABS += [("winTL", w, m) for w in WIN_T for m in range(2)] + [("winL", w, a) for w, a in WIN]


def plan_groups():
    names = []

    def scan(u):
        names.append(("diag", u))
        names.extend(("lvl", u, l, d) for l in range(LEVELS) for d in range(2))
        names.extend([("kT", u), ("dS", u), ("oA", u)])

    def attention(tiles):
        names.extend(("qkT", t) for t in tiles)
        lo, hi = tiles[0] * HB, (tiles[-1] + 1) * HB
        for n in range(lo, hi + 2):
            if n < hi:
                names.append(("sc", n))
            if lo <= n - 1 < hi:
                names.append(("pT", n - 1))
            if n - 2 >= lo and (n - 2) % HB == 0:
                names.append(("oB", (n - 2) // HB))

    def post(b):
        tiles = BATCHES[b]
        names.extend(("oT", t) for t in tiles)
        for q in range(4):
            names.extend(("gate_a", b, 2 * q + m) for m in range(2))
            names.extend(("gate_b", b, 2 * q + m) for m in range(2))
            for m in range(2):
                names.extend([("ra", b, 2 * q + m), ("rb", b, 2 * q + m)])
        names.extend(("y", q, t) for q in range(4) for t in tiles)
        for t in tiles:
            names.extend([("x2T", t), ("h2", t)])
        names.append(("qp", b, 0))
        for m in range(2 * PH):
            if m + 1 < 2 * PH:
                names.append(("qp", b, m + 1))
            names.append(("ss", b, m))

    for n in range(NADA + 1):
        if n < NADA:
            names.append(("ada", n))
        if n:
            names.append(("mod", n - 1))
    names.extend(("xT", t) for t in range(NT))
    names.extend(("winP", w, m) for w in WIN_T for m in range(4))
    names.extend(("win", w, a, 0) for w, a in WIN)
    scan(0)
    attention([0])
    post(0)
    beside = [len(names)]
    names.extend(("winT", w, m) for w in WIN_T for m in range(4))
    names.extend(("win", w, a, t) for w, a in WIN for t in range(1, NT))
    for u in range(1, NT):
        scan(u)
    attention([1, 2, 3, 4])
    post(1)
    beside.append(len(names))
    post(2)
    beside.append(len(names))
    place, used, fulls, n, long = {}, [0] * 6, [0] * 6, 0, 0
    for name in names:
        kind = name[0]
        wide = kind in ("xT", "kT", "dS", "qkT", "oT", "x2T", "h2") or (kind in ("sc", "pT") and name[1] >= HB)
        if kind in ("oA", "oB"):
            banks = (4 + long % 2,)
            long += 1
        else:
            n += wide and n % 2
            banks = (n % 4, n % 4 + 1) if wide else (n % 4,)
            n += len(banks)
        fulls[banks[0]] += 1
        place[name] = (banks, [used[b] for b in banks], fulls[banks[0]])
        for b in banks:
            used[b] += 1

    def settle(at):
        if at + 1 >= len(names):
            return at
        nxt = names[at + 1]
        if nxt[0] == "lvl" and nxt[3] == 0:
            return at + 1
        while names[at + 1][0] in ("pT", "oB"):
            at -= 1
        return at

    slot_at = []
    for t in range(2):
        span = range(beside[t], beside[t + 1])
        reach = np.cumsum([SHARE[names[i][0]] for i in span])
        for k in range(TSLOT):
            at = beside[t] + int(np.searchsorted(reach, (k + 0.01) / TSLOT * reach[-1]))
            if names[at][0] in ("sc", "pT") and k % 2 and t == 0:
                at = max(slot_at[-1], 0)
            slot_at.append(settle(at))
    return names, place, slot_at


NAMES, PLACE, SLOT_AT = plan_groups()
INDEX = {name: i for i, name in enumerate(NAMES)}


def build(nc, x_prompt, x_sample, cols, rows, normf_rows, brow, consts, masks, sel, w_ada, w_in, w_oa, w_ob, w_out,
          w_pq, keysT, uv, state, ckT, cv, y_prompt, y_sample, new_state, new_k, new_v):
    with ExitStack() as ctx:
        def sb(name, shape, dt=F32):
            return ctx.enter_context(nc.sbuf_tensor(name, shape, dt))

        def sem(name):
            return ctx.enter_context(nc.semaphore(name))

        def view(t, at, *dims):
            n = int(np.prod(dims))
            s = t[:, at:at + n]
            if len(dims) == 2:
                return s.rearrange("p (a b) -> p a b", a=dims[0])
            if len(dims) == 3:
                return s.rearrange("p (a b c) -> p a b c", a=dims[0], b=dims[1])
            return s

        XP = sb("XP", [P, D])
        R1 = sb("R1", [P, 4 * D])
        G1L = sb("G1L", [P, D])
        G2 = sb("G2", [P, 2, D])
        EB = sb("EB", [P, 2 * D])
        HL = sb("HL", [P, KD * LAT])
        RW_ = sb("RING", [P, NSLAB * SLOTW])
        RG = sb("RG", [P, 3 * 2 * D])
        PB = sb("PB", [P, 6 * 512])
        AB = sb("AB", [P, 12288])
        HG = sb("HG", [P, 5632])
        ST0 = sb("ST0", [P, 2, HA, P])
        BKV = sb("BKV", [P, NT, 256])
        CO = sb("CO", [P, NCOLS])
        RW = sb("RW", [P, 512 + HB])
        CT = sb("CT", [P, P + 640 + NCAND])
        MK = sb("MK", [P, 15, P], U8)
        condT = sb("condT", [P, 2, KD])
        ADA = sb("ADA", [P, 4, 2, KD])
        AM = sb("AM", [P, 2, 2, KD])
        LB = sb("LB", [P, 2, 6, HA])
        st = sb("st", [P, 32])
        hst = sb("hst", [P, 16])
        ast = sb("ast", [P, 168])
        ZB = sb("ZB", [P, P], BF16)
        idxs = sb("idxs", [P, 2, TOPK], I32)
        gws = sb("gws", [P, 2, TOPK])
        apre = sb("apre", [P, 2, TOPK])
        agel = sb("agel", [P, 2, TOPK])
        wexp = sb("wexp", [P, 2, TOPK])
        ident, mbias, iota = CT[:, 0:P], CT[:, P:P + 640], CT[:, P + 640:P + 640 + NCAND]
        anorm, sink = RW[:, 0:512], RW[:, 512:512 + HB]
        G1P, hTp, hTl = EB[:, 0:D], view(EB, D, KD, P), view(HL, 0, KD, LAT)
        BR = AB[0:2, 6144:6144 + 6 * D].rearrange("p (a b) -> p a b", a=6)
        GR = [AB[0:2, 0:SC_W], AB[0:2, SC_W:2 * SC_W]]
        SEL = AB[0:2, 512:768].rearrange("p (a b) -> p a b", a=2)
        MK4 = view(AB, 4096, 15, P)
        XL = view(R1, 0, 4, D)
        XN1, SQ1 = view(HG, 0, 2, D), view(HG, 2048, D)
        ROT = HG[:, 4352:4864]
        cosT, sinT = view(HG, 4352, 4, HD), view(HG, 4608, 4, HD)
        RP1, RP2 = view(HG, 3072, 640), view(HG, 3712, 640)

        def QU(u):
            return PB[:, 0:512] if u == 0 else AB[:, (u - 1) * 512:u * 512]

        def FU(d, u):
            return PB[:, 512 * (1 + d):512 * (2 + d)] if u == 0 else AB[:, 2048 * (1 + d) + (u - 1) * 512:
                                                                        2048 * (1 + d) + u * 512]

        def by_tile(at_p, at_l):
            return lambda t: PB[:, at_p:at_p + 512] if t == 0 else AB[:, at_l + (t - 1) * 512:at_l + t * 512]

        IV, OA, BQ = by_tile(1536, 6144), by_tile(2048, 8192), by_tile(2560, 10240)
        NST = [PB[:, 0:512], PB[:, 512:1024]]
        HQ = [view(HG, 0, 512), view(HG, 512, 512)]
        HK = [view(HG, 1024, 512), view(HG, 1536, 512)]
        HT = [[view(HG, 2048, 256), view(HG, 2304, 128)], [view(HG, 2432, 256), view(HG, 2688, 128)]]
        HS, HKT, HST, HSQ = view(HG, 2816, 512), view(HG, 3328, 8, P), view(HG, 4352, 2, 3, P), view(HG, 5120, 512)

        def QT(t):
            return HG[:, 0:512] if t == 0 else AB[:, (t - 1) * 512:t * 512]

        def KT(t):
            return HG[:, 512:640] if t == 0 else AB[:, 2048 + (t - 1) * P:2048 + t * P]

        ATT = [[view(R1, i * 1280, 2, 640) for i in range(3)], [view(AB, 2560 + i * 1280, 2, 640) for i in range(3)]]
        CKT, CV = view(HG, 0, 256), view(HG, 256, 2, P)

        NB = [len(t) * P for t in BATCHES]
        OT = [view(HG, 0, KD, P), view(HG, 0, KD, P), view(AB, 4096, KD, NB[2])]
        MT = [view(HG, 1024, KD, P), view(HG, 1024, KD, P), view(AB, 8192, KD, NB[2])]
        SAB = [[view(HG, 2048, 2, P), view(HG, 2304, 2, P)]] * 2 + [[view(HG, 0, 2, NB[2]), view(HG, 768, 2, NB[2])]]
        XN2 = [view(HG, 3072, D), view(HG, 3072, D), view(HG, 1536, D)]
        SQ2 = [view(HG, 4096, D), view(HG, 4096, D), view(AB, 7168, D)]
        QP = [view(HG, 5120, 2, P), view(HG, 5120, 2, P), view(HG, 0, 2, NB[2])]
        X1 = [XP[:, :], AB[:, 3072:4096]] + [HG[:, 2560 + i * D:2560 + (i + 1) * D] for i in range(3)]
        H2 = [PB[:, 0:D], AB[:, 0:D]] + [AB[:, 4096 + i * D:4096 + (i + 1) * D] for i in range(3)]
        SC = [R1[:, 0:2048], AB[:, 1024:3072], AB[:, 8192:10240], AB[:, 10240:12288], R1[:, 0:2048]]

        def h_of(b, k):
            return hTp[:, k, :] if b == 0 else hTl[:, k, (0 if b == 1 else P):(P if b == 1 else LAT)]

        def h_tile(t, k):
            return hTp[:, k, :] if t == 0 else hTl[:, k, (t - 1) * P:t * P]

        GA = [RG[:, i * 2 * D:(i + 1) * 2 * D] for i in range(3)] + [EB[:, :]]
        GB_ = GA + [RW_[:, i * 2 * D:(i + 1) * 2 * D] for i in range(3)] + [HL[:, 0:2 * D]]
        SCR = [R1[:, (2 + i) * D:(3 + i) * D] for i in range(2)]
        DG = view(PB, 1024, 2, P)
        RS, RS2 = view(PB, 1280, 256), view(PB, 1536, 256)
        RV, RI, RIF = view(PB, 1792, 2, TOPK), PB[:, 1824:1856].bitcast(U32), PB[:, 1856:1888]
        RC, RC2, RCI = PB[:, 1888:1938], PB[:, 1940:1990], PB[:, 1992:2042]
        RT, RP, RPF, RX, RE = (PB[:, 2044:2060], PB[:, 2060:2076].bitcast(U32), PB[:, 2076:2092], PB[:, 2092:2108],
                               PB[:, 2108:2124])
        RM, RSUM, RR = PB[:, 2124:2125], PB[:, 2125:2126], PB[:, 2126:2127]
        REQ = view(PB, 2128, TOPK, NCAND)

        PA = ctx.enter_context(nc.psum_tensor("pa", [P, 4 * 512], F32))
        PO = ctx.enter_context(nc.psum_tensor("po", [P, 2 * 512], F32))
        PL = ctx.enter_context(nc.psum_tensor("pl", [P, 2 * 512], F32))

        def psum(name):
            banks = PLACE[name][0]
            return (PA[:, 512 * banks[0]:512 * (banks[-1] + 1)] if banks[0] < 4
                    else PO[:, 512 * (banks[0] - 4):512 * (banks[0] - 3)])

        full = [sem(f"full{i}") for i in range(6)]
        free = [sem(f"free{i}") for i in range(6)]
        slab_in = [sem(f"slab_in{i}") for i in range(NSLAB)]
        x_in, small_in, misc_in, xr_in = sem("x_in"), sem("small_in"), sem("misc_in"), sem("xr_in")
        act_step, dve_step, pool_step = sem("act_step"), sem("dve_step"), sem("pool_step")
        cond_ready, am_ready, mk_ready, rot_in = sem("cond_ready"), sem("am_ready"), sem("mk_ready"), sem("rot_in")
        ssq_ready, rms_ready, xn_ready, hT_ready = sem("ssq_ready"), sem("rms_ready"), sem("xn_ready"), sem("hT_ready")
        grow_ready, gate_ready = sem("grow_ready"), sem("gate_ready")
        lbx_ready, lbe_ready = sem("lbx_ready"), sem("lbe_ready")
        q_ready, sig_ready, f_ready = sem("q_ready"), sem("sig_ready"), sem("f_ready")
        win_ready = {w: sem(f"win_ready{w}") for w in (W_I, W_AG, W_BQ, W_BKV)}
        rope_ready = sem("rope_ready")
        hg_ready = [sem("hgf_ready"), sem("hgb_ready")]
        hs_ready, kT_ready, st_ready = sem("hs_ready"), sem("kT_ready"), sem("st_ready")
        osq_ready, ossq_ready, orms_ready, oa_ready = sem("osq_ready"), sem("ossq_ready"), sem("orms_ready"), sem("oa_ready")
        nst_ready, ctx_in = sem("nst_ready"), sem("ctx_in")
        qkT_ready, sm_ready, p_ready, pT_ready, ob_ready = (sem("qkT_ready"), sem("sm_ready"), sem("p_ready"),
                                                            sem("pT_ready"), sem("ob_ready"))
        oT_ready, sig2_ready, m_ready = sem("oT_ready"), sem("sig2_ready"), sem("m_ready")
        h2T_ready, h2_ready, qp_ready = sem("h2T_ready"), sem("h2_ready"), sem("qp_ready")
        kv_out, state_out, y_out, nf_in, zb_ready = (sem("kv_out"), sem("state_out"), sem("y_out"), sem("nf_in"),
                                                     sem("zb_ready"))
        U0, V0 = 2, 8
        ga_in = [sem(f"ga_in{i}") for i in range(NGA)]
        gb_in = [sem(f"gb_in{i}") for i in range(NGB)]
        go, waited = sem("go"), sem("waited")
        idx_ready, logit_ready, expo_ready, gw_ready = sem("idx_ready"), sem("logit_ready"), sem("expo_ready"), sem("gw_ready")
        route_step, u_done, gel_done, w_done, dg_done, v_done = (sem("route_step"), sem("u_done"), sem("gel_done"),
                                                                sem("w_done"), sem("dg_done"), sem("v_done"))
        acc_closed, acc_read, fss_ready, frt_ready, y_ready = (sem("acc_closed"), sem("acc_read"), sem("fss_ready"),
                                                              sem("frt_ready"), sem("y_ready"))

        class Steps:

            def __init__(self, eng, s):
                self.eng, self.s, self.n = eng, s, 0

            def __call__(self, ins, *signals):
                self.n += 1
                ins.then_inc(self.s, 1)
                self.eng.wait_ge(self.s, self.n)
                for x in signals:
                    self.eng.sem_inc(x, 1)

        class Beside:

            def __init__(self, slot, shift):
                self.slot, self.shift, self.next, self.end = slot, shift, 0, 0

            def place(self, n):
                n += self.shift
                return SLOT_AT[min(max(n, self.end - TSLOT), self.end)] if n < self.end else len(NAMES)

            def before(self, name):
                while self.next < self.end and self.place(self.next) < INDEX[name]:
                    self.slot(self.next)
                    self.next += 1

            def open(self, t):
                self.end = (t + 1) * TSLOT

            def rest(self):
                while self.next < self.end:
                    self.slot(self.next)
                    self.next += 1

        def wait_full(eng, name):
            banks, _, count = PLACE[name]
            eng.wait_ge(full[banks[0]], count)
            return psum(name)

        def freed(name):
            return [free[b] for b in PLACE[name][0]]

        def unit_block(u, b):
            return (0, b) if u == 0 else (b + 1, u - 1)

        def score_span(t):
            return (P, 2 * P) if t == 0 else (P if t == 1 else 0, 4 * P if t == NT - 1 else 5 * P)

        def half_update(d, l, mul, u):
            B = 1 << l
            T = FU(d, u) if l == 0 else HT[d][(l - 1) % 2][:, 0:512 >> l]
            T2 = T.rearrange("p (n a) -> p n a", a=2)
            q = HQ[d].rearrange("p (n a b) -> p n a b", a=2, b=B)
            k = HK[d].rearrange("p (n a b) -> p n a b", a=2, b=B)
            n = 256 // B
            lo, hi = T2[:, :, 0:1].to_broadcast([P, n, B]), T2[:, :, 1:2].to_broadcast([P, n, B])
            qh, kh = (1, 0) if d == 0 else (0, 1)
            yield mul(q[:, :, qh], q[:, :, qh], lo if d == 0 else hi)
            yield mul(k[:, :, kh], k[:, :, kh], hi if d == 0 else lo)
            yield mul(HT[d][l % 2][:, 0:n], T2[:, :, 0], T2[:, :, 1])

        slab_turn, counts = {}, [0] * NSLAB
        for n, key in enumerate(SLABS):
            counts[n % NSLAB] += 32 if key[0] in ("wo", "wpq") else 16
            slab_turn[key] = (n % NSLAB, counts[n % NSLAB])

        block = ctx.enter_context(nc.Block())

        @block.sync
        def _(sp):
            def last_use(key):
                kind = key[0]
                if kind == "ada":
                    return key
                if kind in ("winT", "winTL"):
                    return ("winP" if kind == "winT" else "winT", key[1], 2 * key[2] + 1)
                if kind in ("win", "winL"):
                    return ("win", key[1], key[2], 0 if kind == "win" else NT - 1)
                b, q = key[1:]
                return {"gate_a": ("gate_a", b, 2 * q + 1), "gate_b": ("gate_b", b, 2 * q + 1),
                        "wo": ("rb", b, 2 * q + 1), "wout": ("y", q, BATCHES[b][-1]),
                        "wpq": ("ss", b, 2 * q + 1)}[kind]

            sp.dma_start(CO[:], cols).then_inc(small_in, 16)
            sp.dma_start(CT[:], consts[:, 0:P + 640 + NCAND]).then_inc(small_in, 16)
            sp.dma_start(SEL, sel).then_inc(small_in, 16)
            sp.dma_start(BR, brow).then_inc(small_in, 16)
            for n, key in enumerate(SLABS):
                if n >= NSLAB:
                    wait_full(sp, last_use(SLABS[n - NSLAB]))
                at = RW_[:, (n % NSLAB) * SLOTW:(n % NSLAB + 1) * SLOTW]
                s = slab_in[n % NSLAB]
                kind = key[0]
                if kind == "wo":
                    for i, w in enumerate((w_oa, w_ob)):
                        sp.dma_start(at[:, i * 1024:(i + 1) * 1024].rearrange("p (k n) -> p k n", k=4),
                                     w.rearrange("(k p) n -> p k n", p=P)[:, :, key[2] * SC_W:(key[2] + 1) * SC_W]
                                     ).then_inc(s, 16)
                else:
                    if kind == "ada":
                        w, c = w_ada, ADA_SEGS[key[1] // 4] * D + key[1] % 4 * SC_W
                    elif kind in ("win", "winL", "winT", "winTL"):
                        w, c = w_in, key[1] + key[2] * SC_W
                    elif kind in ("gate_a", "gate_b"):
                        w, c = w_in, (W_GA if kind == "gate_a" else W_GB) + key[2] * SC_W
                    else:
                        w, c = (w_out if kind == "wout" else w_pq), key[2] * SC_W
                    sp.dma_start(at[:, 0:SLAB].rearrange("p (k n) -> p k n", k=KD),
                                 w.rearrange("(k p) n -> p k n", p=P)[:, :, c:c + SC_W]).then_inc(s, 16)
                    if kind == "wpq":
                        sp.dma_start(at[:, SLAB:SLOTW], keysT[:, key[2] * 2 * NKEYS:(key[2] + 1) * 2 * NKEYS]
                                     ).then_inc(s, 16)
                if n == 2:
                    sp.dma_start(XP[:], x_prompt).then_inc(x_in, 16)
                    sp.dma_start(XL, x_sample.rearrange("(t p) d -> p t d", p=P)).then_inc(x_in, 16)
                if n == NADA:
                    sp.dma_start(RW[:], rows).then_inc(misc_in, 16)
                    sp.dma_start(MK4, masks).then_inc(misc_in, 16)
                    sp.dma_start(ST0[:], state.rearrange("a h k v -> k a h v")).then_inc(misc_in, 16)
            for t in range(NT):
                sp.wait_ge(y_ready, t + 1)
                dst = y_prompt if t == 0 else y_sample[(t - 1) * P:t * P, :]
                sp.dma_start(dst, X1[t]).then_inc(y_out, 16)
            sp.wait_ge(y_out, 16 * NT)
            sp.wait_ge(kv_out, 32)
            sp.wait_ge(state_out, 32)

        @block.tensor
        def _(pe):
            order = iter(NAMES)

            def v_slot(n, k, bufs):
                pe.wait_ge(dg_done, n - 2 * TSLOT + 1)
                for c in range(2):
                    last = nc.tensor.matmul(PL[:, c * 512:(c + 1) * 512], DG[:, k % 2, :],
                                            bufs[k % len(bufs)][:, D + c * 512:D + (c + 1) * 512], start=False,
                                            stop=False, skip_group_check=True)
                last.then_inc(v_done, 1)

            def start(name):
                assert next(order) == name, name
                for b, turn in zip(*PLACE[name][:2]):
                    if turn:
                        pe.wait_ge(free[b], turn)
                return psum(name)

            def finish(name, ins):
                ins.then_inc(full[PLACE[name][0][0]], 1)

            def slab(*key):
                slot, count = slab_turn[key]
                pe.wait_ge(slab_in[slot], count)
                return RW_[:, slot * SLOTW:(slot + 1) * SLOTW]

            def chunks(w):
                return w[:, 0:SLAB].rearrange("p (k n) -> p k n", k=KD)

            def mm(out, l, r, s=True, e=True):
                return nc.tensor.matmul(out, l, r, start=s, stop=e)

            def tr(out, i):
                return nc.tensor.transpose(out, i, ident)

            pe.wait_ge(small_in, 64)
            pe.wait_ge(cond_ready, 1)
            for n in range(NADA + 1):
                if n < NADA:
                    w = chunks(slab("ada", n))
                    ps = start(("ada", n))
                    for k in range(KD):
                        last = mm(ps[0:2, 0:SC_W], condT[:, :, k], w[:, k, :], k == 0, k == KD - 1)
                    finish(("ada", n), last)
                if n:
                    pe.wait_ge(grow_ready, n)
                    ps = start(("mod", n - 1))
                    row = GR[(n - 1) % 2]
                    if ADA_SEGS[(n - 1) // 4] in GATE_SEGS:
                        for c in range(2):
                            last = mm(ps[:, c * SC_W:(c + 1) * SC_W], SEL[:, c, :], row)
                    else:
                        for m in range(2):
                            last = nc.tensor.transpose(ps[:, 2 * m:2 * m + 2], row[:, m * P:(m + 1) * P],
                                                       ident[0:2, 0:2])
                    finish(("mod", n - 1), last)

            for t in range(NT):
                pe.wait_ge(xn_ready, t + 1)
                ps = start(("xT", t))
                for k in range(KD):
                    last = tr(ps[:, k * P:(k + 1) * P], XN1[:, t % 2, k * P:(k + 1) * P])
                finish(("xT", t), last)
            pe.wait_ge(hT_ready, NT)
            def win_turned(kind, name, h, N):
                for wc in WIN_T:
                    for m in range(4):
                        w = chunks(slab(kind, wc, m // 2))[:, :, (m % 2) * P:(m % 2 + 1) * P]
                        ps = start((name, wc, m))
                        for k in range(KD):
                            last = mm(ps[:, 0:N], w[:, k, :], h[:, k, :], k == 0, k == KD - 1)
                        finish((name, wc, m), last)

            win_turned("winT", "winP", hTp, P)

            def win(kind, tiles):
                for wc, a in WIN:
                    w = chunks(slab(kind, wc, a))
                    for t in tiles:
                        ps = start(("win", wc, a, t))
                        for k in range(KD):
                            last = mm(ps[:, 0:SC_W], h_tile(t, k), w[:, k, :], k == 0, k == KD - 1)
                        finish(("win", wc, a, t), last)

            win("win", [0])
            pe.wait_ge(win_ready[W_I], 2)
            pe.wait_ge(misc_in, 48)

            def scan(u):
                bl = [slice(b * P, (b + 1) * P) for b in range(4)]
                for d in range(2):
                    pe.wait_ge(hg_ready[d], (LEVELS + 1) * u + 1)
                ps = start(("diag", u))
                for b in range(4):
                    mm(ps[:, bl[b]], HK[0][:, bl[b]], QU(u)[:, bl[b]], True, False)
                    last = mm(ps[:, bl[b]], HK[1][:, bl[b]], QU(u)[:, bl[b]], False, True)
                finish(("diag", u), last)
                for l in range(LEVELS):
                    for d in range(2):
                        pe.wait_ge(hg_ready[d], (LEVELS + 1) * u + l + 1)
                        ps = start(("lvl", u, l, d))
                        for b in range(4):
                            last = mm(ps[:, bl[b]], HK[d][:, bl[b]], HQ[d][:, bl[b]])
                        finish(("lvl", u, l, d), last)
                for d in range(2):
                    pe.wait_ge(hg_ready[d], (LEVELS + 1) * (u + 1))
                ps = start(("kT", u))
                for d in range(2):
                    for b in range(4):
                        last = tr(ps[:, (4 * d + b) * P:(4 * d + b + 1) * P], HK[d][:, bl[b]])
                finish(("kT", u), last)
                pe.wait_ge(kT_ready, u + 1)
                ps = start(("dS", u))
                for d in range(2):
                    for b in range(4):
                        t, h = unit_block(u, b)
                        last = mm(ps[:, (4 * d + b) * P:(4 * d + b + 1) * P], HKT[:, 4 * d + b, :],
                                  IV(t)[:, h * P:(h + 1) * P])
                finish(("dS", u), last)
                pe.wait_ge(hs_ready, u + 1)
                pe.wait_ge(st_ready, u + 1)
                ps = start(("oA", u))
                for b in range(4):
                    t, h = unit_block(u, b)
                    last = mm(ps[:, bl[b]], HS[:, bl[b]], IV(t)[:, h * P:(h + 1) * P], True, u == 0)
                    if u:
                        for d in range(2):
                            n = b if d == 0 else 3 - b
                            s0 = ST0[:, d, h, :] if n == 0 else HST[:, d, n - 1, :]
                            last = mm(ps[:, bl[b]], HQ[d][:, bl[b]], s0, False, d == 1)
                finish(("oA", u), last)

            def key_blocks(t):
                if t == 0:
                    return [(P, 0)]
                return [(c, k) for c, k in ((0, t - 1), (P, t), (2 * P, "c0"), (3 * P, "c1"), (4 * P, t + 1))
                        if not (k == 0 or k == NT)]

            def attention(tiles):
                _, PR, PT = ATT[tiles[0] > 0]
                if tiles[0]:
                    pe.wait_ge(rope_ready, 4)
                pe.wait_ge(win_ready[W_BKV], NT if tiles[0] else 1)
                pe.wait_ge(win_ready[W_BQ], 2 * NT if tiles[0] else 2)
                for t in tiles:
                    ps = start(("qkT", t))
                    for j in range(4):
                        tr(ps[:, j * P:(j + 1) * P], BQ(t)[:, j * P:(j + 1) * P])
                    last = tr(ps[:, 512:640], BKV[:, t, 0:P])
                    finish(("qkT", t), last)
                pe.wait_ge(qkT_ready, tiles[-1] + 1)
                if tiles[0]:
                    pe.wait_ge(ctx_in, 32)

                def scores(n):
                    t, h = HEADS[n]
                    g, j = h // 4, h % 4
                    r = slice(g * HD, (g + 1) * HD)
                    ps = start(("sc", n))
                    q = QT(t)[r, j * P:(j + 1) * P]
                    if t > 1:
                        mm(ps[:, 0:P], q, KT(t - 1)[r, :])
                    last = mm(ps[:, P:2 * P], q, KT(t)[r, :])
                    if t:
                        last = mm(ps[:, 2 * P:4 * P], q, CKT[r, :])
                        if t < NT - 1:
                            last = mm(ps[:, 4 * P:5 * P], q, KT(t + 1)[r, :])
                    finish(("sc", n), last)

                def turn_p(n):
                    pe.wait_ge(p_ready, n + 1)
                    ps = start(("pT", n))
                    for c, _ in key_blocks(HEADS[n][0]):
                        last = tr(ps[:, c:c + P], PR[:, n % 2, c:c + P])
                    finish(("pT", n), last)

                def values(n):
                    t, h = HEADS[n]
                    g = h // 4
                    if h == 0:
                        start(("oB", t))
                    pe.wait_ge(pT_ready, n + 1)
                    ps = psum(("oB", t))
                    kb = key_blocks(t)
                    for i, (c, k) in enumerate(kb):
                        v = (CV[:, int(k[1]), g * HD:(g + 1) * HD] if isinstance(k, str)
                             else BKV[:, k, P + g * HD:P + (g + 1) * HD])
                        last = mm(ps[:, h * HD:(h + 1) * HD], PT[:, n % 2, c:c + P], v, i == 0, i == len(kb) - 1)
                    if h == HB - 1:
                        finish(("oB", t), last)

                lo, hi = tiles[0] * HB, (tiles[-1] + 1) * HB
                for n in range(lo, hi + 2):
                    if n < hi:
                        scores(n)
                    if lo <= n - 1 < hi:
                        turn_p(n - 1)
                    if n - 2 >= lo:
                        values(n - 2)

            def post(b):
                tiles, N = BATCHES[b], NB[b]
                pe.wait_ge(oa_ready, 1 if b == 0 else NT)
                for t in tiles:
                    pe.wait_ge(ob_ready, t + 1)
                    ps = start(("oT", t))
                    for k in range(4):
                        tr(ps[:, k * P:(k + 1) * P], OA(t)[:, k * P:(k + 1) * P])
                    for k in range(4):
                        last = tr(ps[:, (4 + k) * P:(5 + k) * P], BQ(t)[:, k * P:(k + 1) * P])
                    finish(("oT", t), last)
                for q in range(4):
                    for name in ("gate_a", "gate_b"):
                        w = chunks(slab(name, b, q))
                        for m in range(2):
                            ps = start((name, b, 2 * q + m))
                            for k in range(KD):
                                last = mm(ps[:, 0:N], w[:, k, m * P:(m + 1) * P], h_of(b, k), k == 0, k == KD - 1)
                            finish((name, b, 2 * q + m), last)
                    w = slab("wo", b, q)[:, 0:SLAB].rearrange("p (a k n) -> p a k n", a=2, k=4)
                    if q == 0:
                        pe.wait_ge(oT_ready, tiles[-1] + 1)
                    for m in range(2):
                        for a, name in enumerate(("ra", "rb")):
                            ps = start((name, b, 2 * q + m))
                            for k in range(4):
                                last = mm(ps[:, 0:N], w[:, a, k, m * P:(m + 1) * P], OT[b][:, 4 * a + k, :],
                                          k == 0, k == 3)
                            finish((name, b, 2 * q + m), last)
                pe.wait_ge(m_ready, KD * (b + 1))
                for q in range(4):
                    w = chunks(slab("wout", b, q))
                    for i, t in enumerate(tiles):
                        ps = start(("y", q, t))
                        for k in range(KD):
                            last = mm(ps[:, 0:SC_W], MT[b][:, k, i * P:(i + 1) * P], w[:, k, :], k == 0, k == KD - 1)
                        finish(("y", q, t), last)
                for t in tiles:
                    pe.wait_ge(xn_ready, NT + t + 1)
                    ps = start(("x2T", t))
                    for k in range(KD):
                        last = tr(ps[:, k * P:(k + 1) * P], XN2[b][:, k * P:(k + 1) * P])
                    finish(("x2T", t), last)
                    pe.wait_ge(h2T_ready, t + 1)
                    ps = start(("h2", t))
                    for k in range(KD):
                        last = tr(ps[:, k * P:(k + 1) * P], h_tile(t, k))
                    finish(("h2", t), last)

                def queries(m):
                    w = chunks(slab("wpq", b, m // 2))
                    ps = start(("qp", b, m))
                    for k in range(KD):
                        last = mm(ps[:, 0:N], w[:, k, (m % 2) * P:(m % 2 + 1) * P], h_of(b, k), k == 0, k == KD - 1)
                    finish(("qp", b, m), last)

                queries(0)
                for m in range(2 * PH):
                    if m + 1 < 2 * PH:
                        queries(m + 1)
                    keys = slab("wpq", b, m // 2)[:, SLAB + (m % 2) * NKEYS:SLAB + (m % 2 + 1) * NKEYS]
                    pe.wait_ge(qp_ready, 2 * PH * b + m + 1)
                    ps = start(("ss", b, m))
                    for i in range(len(tiles)):
                        last = mm(ps[:, i * P:(i + 1) * P], QP[b][:, m % 2, i * P:(i + 1) * P], keys)
                    finish(("ss", b, m), last)

            def edge(start_, signal=None):
                for c in range(8):
                    last = nc.tensor.matmul(PL[:, c * P:(c + 1) * P], ZB[:, :], ZB[:, :], start=start_ and c % 4 == 0,
                                            stop=not start_, skip_group_check=True)
                if signal is not None:
                    last.then_inc(signal, 1)

            scan(0)
            attention([0])
            post(0)
            win_turned("winTL", "winT", hTl, LAT)
            win("winL", range(1, NT))
            pe.wait_ge(win_ready[W_I], 2 * NT)
            for u in range(1, NT):
                scan(u)
            attention([1, 2, 3, 4])
            post(1)
            post(2)
            pe.wait_ge(zb_ready, 1)
            for t in range(2, NT):
                pe.wait_ge(acc_read, t)
                edge(True)

                def pass_(p):
                    for k in range(HSLOTS):
                        v_slot(t * TSLOT + p * HSLOTS + k, k, GB_)

                with pe.Fori(0, 3) as p:
                    pass_(p)
                pass_(3)
                edge(False, acc_closed)

        @block.scalar
        def _(act):
            step = Steps(act, act_step)
            A = nc.scalar.activation

            def expos(j):
                act.wait_ge(logit_ready, j + 1)
                A(RE, RT, ACT.Exp, bias=RM, accum_out=RSUM).then_inc(expo_ready, 1)

            def w_slot(n, j, k, par, route, diagonal):
                act.wait_ge(u_done, n + 1 + U0)
                A(agel[:, par, k:k + 1], apre[:, par, k:k + 1], ACT.Gelu).then_inc(gel_done, 1)
                if k == 0:
                    act.wait_ge(gw_ready, j + 1)
                act.wait_ge(gel_done, n + 1)
                if not diagonal:
                    act.wait_ge(v_done, n - 1 + V0)
                A(wexp[:, par, k:k + 1], agel[:, par, k:k + 1], ACT.Copy, scale=gws[:, par, k:k + 1]).then_inc(w_done, 1)
                if diagonal:
                    act.wait_ge(w_done, n + 1)
                    act.wait_ge(v_done, n - 1 + V0)
                    A(DG[:, k % 2, :], ident, ACT.Copy, scale=wexp[:, par, k:k + 1]).then_inc(dg_done, 1)
                if k == EXPO_AT and route:
                    expos(j + 1)

            beside = Beside(lambda n: w_slot(n, n // TOPK, n % TOPK, n // TOPK % 2, (n // TOPK) % PH < PH - 1, False), 0)

            def group(name):
                beside.before(name)
                return wait_full(act, name)

            act.wait_ge(small_in, 64)
            step(A(condT[:].rearrange("p c k -> p (c k)"), CO[:, C_COND:C_COND + 16], ACT.Silu), cond_ready)
            act.wait_ge(lbx_ready, 1)
            step(A(LB[:, :, 2:4, :], LB[:, :, 0:2, :], ACT.Exp), lbe_ready)
            for n in range(NADA):
                s, c0 = ADA_SEGS[n // 4], (n % 4) * SC_W
                if s in GATE_SEGS:
                    ps = group(("mod", n))
                    if s == GATE_SEGS[0]:
                        step(A(G1P[:, c0:c0 + SC_W], ps[:, 0:SC_W], ACT.Copy))
                        step(A(G1L[:, c0:c0 + SC_W], ps[:, SC_W:2 * SC_W], ACT.Copy), *freed(("mod", n)), gate_ready)
                    else:
                        step(A(G2[:, :, c0:c0 + SC_W], ps[:, 0:512].rearrange("p (c n) -> p c n", c=2), ACT.Copy),
                             *freed(("mod", n)), gate_ready)

            def root(n):
                act.wait_ge(ssq_ready, n + 1)
                step(A(st[:, 16 + n % NT:17 + n % NT], st[:, 8 + n % NT:9 + n % NT], ACT.Sqrt), rms_ready)

            def turned(name, t, which, ready):
                ps = group((name, t))
                c = 0 if t == 0 else 1
                for k in range(KD):
                    step(A(h_tile(t, k), ps[:, k * P:(k + 1) * P], ACT.Identity, scale=AM[:, which, c, k:k + 1],
                           bias=ADA[:, 1 + which, c, k:k + 1]))
                for x in freed((name, t)) + [ready]:
                    act.sem_inc(x, 1)

            for t in range(NT):
                root(t)
            act.wait_ge(am_ready, 3)
            for t in range(NT):
                turned("xT", t, 0, hT_ready)
            WT = ((W_Q, QU, ACT.Silu, q_ready), (W_FF, lambda u: FU(0, u), ACT.Sigmoid, sig_ready),
                  (W_FB, lambda u: FU(1, u), ACT.Sigmoid, sig_ready))
            for wc, dst, fn, ready in WT:
                for m in range(4):
                    ps = group(("winP", wc, m))
                    step(A(dst(0)[:, m * P:(m + 1) * P], ps[:, 0:P], fn), *freed(("winP", wc, m)), ready)

            def win(wc, a, tiles):
                fn = ACT.Silu if wc == W_AG else ACT.Copy
                for t in tiles:
                    ps = group(("win", wc, a, t))
                    i = ps[:, 0:SC_W]
                    if wc == W_BKV:
                        o = BKV[:, t, :]
                    elif wc == W_BQ:
                        o = BQ(t).rearrange("p (j g d) -> p g j d", j=4, g=GB)[:, a]
                        i = i.rearrange("p (j d) -> p j d", j=4)
                    else:
                        o = (IV if wc == W_I else OA)(t)[:, a * SC_W:(a + 1) * SC_W]
                    step(A(o, i, fn), *freed(("win", wc, a, t)), win_ready[wc])

            for wc, a in WIN:
                win(wc, a, [0])

            def scan(u):
                ps = group(("kT", u))
                step(A(HKT.rearrange("p a b -> p (a b)"), ps, ACT.Copy), *freed(("kT", u)), kT_ready)
                ps = group(("oA", u))
                step(A(HSQ, ps, ACT.Square), osq_ready)
                act.wait_ge(ossq_ready, u + 1)
                step(A(hst[:, 4:8], hst[:, 0:4], ACT.Sqrt), orms_ready)

            def attention(tiles):
                SM, PR, _ = ATT[tiles[0] > 0]
                act.wait_ge(oa_ready, 1 if tiles[0] == 0 else NT)
                if tiles[0]:
                    act.dma_start(CKT, ckT).then_inc(ctx_in, 16)
                    act.dma_start(CV, cv.rearrange("(b p) n -> p b n", p=P)).then_inc(ctx_in, 16)
                for t in tiles:
                    ps = group(("qkT", t))
                    step(A(QT(t), ps[:, 0:512], ACT.Copy))
                    step(A(KT(t), ps[:, 512:640], ACT.Copy), *freed(("qkT", t)), qkT_ready)
                lo_, hi_ = tiles[0] * HB, (tiles[-1] + 1) * HB
                for n in range(lo_, hi_):
                    t, h = HEADS[n]
                    lo, hi = score_span(t)
                    beside.before(("pT", n))
                    act.wait_ge(sm_ready, n + 1)
                    if n >= lo_ + 2:
                        wait_full(act, ("pT", n - 2))
                    step(A(PR[:, n % 2, lo:hi], SM[:, n % 2, lo:hi], ACT.Exp, bias=ast[:, 40 + n:41 + n], scale=SCALE,
                           accum_out=ast[:, 80 + n:81 + n]))
                    step(A(ast[:, 120 + n:121 + n], sink[:, h:h + 1], ACT.Exp, bias=ast[:, 40 + n:41 + n]), p_ready)

            def post(b):
                tiles, N = BATCHES[b], NB[b]
                wait_full(act, ("oB", 0 if b == 0 else NT - 1))
                if b == 1:
                    act.wait_ge(ob_ready, NT)
                    act.dma_start(X1[1], x_sample[0:P, :]).then_inc(xr_in, 16)
                if b == 2:
                    wait_full(act, ("ss", 1, 2 * PH - 1))
                    for t in tiles:
                        act.dma_start(X1[t], x_sample[(t - 1) * P:t * P, :]).then_inc(xr_in, 16)
                for i, t in enumerate(tiles):
                    ps = group(("oT", t))
                    step(A(OT[b][:, :, i * P:(i + 1) * P], ps.rearrange("p (k n) -> p k n", k=KD), ACT.Copy),
                         *freed(("oT", t)), oT_ready)
                for q in range(4):
                    if q:
                        beside.before(("rb", b, 2 * q - 1))
                        act.wait_ge(m_ready, KD * b + 2 * q)
                    for a, name in enumerate(("gate_a", "gate_b")):
                        for m in range(2):
                            ps = group((name, b, 2 * q + m))
                            step(A(SAB[b][a][:, m, :], ps[:, 0:N], ACT.Sigmoid), *freed((name, b, 2 * q + m)), sig2_ready)
                for i, t in enumerate(tiles):
                    beside.before(("x2T", t))
                    root(NT + t)
                    turned("x2T", t, 1, h2T_ready)
                    if t == 0:
                        act.wait_ge(state_out, 32)
                    ps = group(("h2", t))
                    step(A(H2[t], ps, ACT.Copy), *freed(("h2", t)), h2_ready)
                for m in range(2 * PH):
                    ps = group(("qp", b, m))
                    if m >= 2:
                        wait_full(act, ("ss", b, m - 2))
                    step(A(QP[b][:, m % 2, :], ps[:, 0:N], ACT.Copy), *freed(("qp", b, m)), qp_ready)

            def tile_end(t):
                act.wait_ge(u_done, (t + 1) * TSLOT + U0)
                act.dma_start(SCR[1], normf_rows).then_inc(nf_in, 16)
                act.wait_ge(fss_ready, t + 1)
                A(st[:, 30:31], st[:, 29:30], ACT.Sqrt).then_inc(frt_ready, 1)

            scan(0)
            attention([0])
            post(0)
            expos(0)
            beside.open(0)
            act.wait_ge(mk_ready, 1)
            for wc, dst, fn, ready in WT:
                for m in range(4):
                    ps = group(("winT", wc, m))
                    step(A(dst(1 + m), ps[:, 0:LAT], fn), *freed(("winT", wc, m)), ready)
            for wc, a in WIN:
                win(wc, a, range(1, NT))
            for u in range(1, NT):
                scan(u)
            attention([1, 2, 3, 4])
            post(1)
            beside.rest()
            expos(PH)
            tile_end(0)
            beside.open(1)
            post(2)
            beside.rest()
            expos(2 * PH)
            tile_end(1)
            for t in range(2, NT):
                def pass_(p, last):
                    for h in range(2):
                        j = t * PH + p * 2 + h
                        for k in range(TOPK):
                            w_slot(j * TOPK + k, j, k, h, not (last and h and t == NT - 1), True)

                with act.Fori(0, 3) as p:
                    pass_(p, False)
                pass_(3, True)
                tile_end(t)

        @block.gpsimd
        def _(pool):
            step = Steps(pool, pool_step)

            def gather(n, k, par, bufs, sems, slot_wait):
                if k == 0:
                    pool.wait_ge(idx_ready, slot_wait[1])
                    pool.sem_inc(go, 1)
                pool.wait_ge(v_done, slot_wait[0])
                pool.sem_inc(go, 1)
                b = (par * TOPK + k) % len(bufs)
                nc.gpsimd.indirect_dma_start(
                    out=bufs[b], out_offset=None, in_=uv,
                    in_offset=bass.IndirectOffsetOnAxis(ap=idxs[:, par, k:k + 1], axis=0)).then_inc(sems[b], 16)

            beside = Beside(lambda n: gather(n, n % TOPK, n // TOPK % 2, GA, ga_in, (n - NGA + 1 + V0, n // TOPK + 1)),
                            -POOL_LEAD)
            pool.memset(ZB[:], 0.0).then_inc(zb_ready, 1)
            pool.wait_ge(win_ready[W_BKV], 1)
            pool.dma_start(new_k, BKV[:, 0, 0:P]).then_inc(kv_out, 16)
            pool.dma_start(new_v, BKV[:, 0, P:2 * P]).then_inc(kv_out, 16)
            pool.wait_ge(f_ready, 2)
            pool.wait_ge(q_ready, 4)

            def mul(o, a, b):
                return nc.gpsimd.tensor_tensor(o, a, b, ALU.mult)

            def scan(u):
                if u > 1:
                    wait_full(pool, ("oA", u - 1))
                step(nc.gpsimd.tensor_scalar(HK[1], FU(1, u), -1.0, 1.0, ALU.mult, ALU.add))
                step(mul(HQ[1], QU(u), FU(1, u)), hg_ready[1])
                for l in range(LEVELS):
                    beside.before(("lvl", u, l, 1))
                    wait_full(pool, ("lvl", u, l, 1))
                    for ins in half_update(1, l, mul, u):
                        step(ins)
                    pool.sem_inc(hg_ready[1], 1)

            scan(0)
            pool.wait_ge(nst_ready, 1)
            for d in range(2):
                pool.dma_start(new_state[d].rearrange("h k v -> k h v"),
                               NST[d].rearrange("p (h v) -> p h v", h=HA)).then_inc(state_out, 16)
            wait_full(pool, ("ss", 0, 2 * PH - 1))
            pool.sem_inc(v_done, V0)
            beside.open(0)
            pool.dma_start(ROT, consts[:, P + 640 + NCAND:]).then_inc(rot_in, 16)
            pool.wait_ge(rot_in, 16)
            for t in range(1, NT):
                beside.before(("win", W_I, 0, t))
                pool.wait_ge(win_ready[W_BQ], NT + t + 1)
                pool.wait_ge(win_ready[W_BKV], t + 1)
                for src, n, at in ((BQ(t), HB, 0), (BKV[:, t, 0:P], GB, 512)):
                    r1 = RP1[:, at:at + n * HD].rearrange("p (h d) -> p h d", h=n)
                    r2 = RP2[:, at:at + n * HD].rearrange("p (h f d) -> p h f d", h=n, f=2)
                    s3 = src.rearrange("p (h d) -> p h d", h=n)
                    s4 = src.rearrange("p (h f d) -> p h f d", h=n, f=2)
                    step(nc.gpsimd.tensor_tensor(r1, s3, cosT[:, t - 1, :].unsqueeze(1).to_broadcast([P, n, HD]),
                                                 ALU.mult))
                    sn = sinT[:, t - 1, :].rearrange("p (f d) -> p f d", f=2)
                    for a in range(2):
                        step(nc.gpsimd.tensor_tensor(
                            r2[:, :, :, a * 16:(a + 1) * 16], s4[:, :, :, (1 - a) * 16:(2 - a) * 16],
                            sn[:, :, a * 16:(a + 1) * 16].unsqueeze(1).to_broadcast([P, n, 2, 16]), ALU.mult))
                    step(nc.gpsimd.tensor_tensor(src, RP1[:, at:at + n * HD], RP2[:, at:at + n * HD], ALU.add))
                pool.sem_inc(rope_ready, 1)
            pool.wait_ge(f_ready, 4)
            pool.wait_ge(q_ready, 8)
            for u in range(1, NT):
                scan(u)
            beside.rest()
            beside.open(1)
            beside.rest()
            pool.wait_ge(v_done, 2 * TSLOT + V0)
            wait_full(pool, ("ss", 2, 2 * PH - 1))
            for t in range(2, NT):
                def pass_(p):
                    for h in range(2):
                        j = t * PH + p * 2 + h
                        for k in range(TOPK):
                            n = j * TOPK + k
                            gather(n, k, h, GB_, gb_in, (n - NGB + 1 + V0, j + 1))

                with pool.Fori(0, 3) as p:
                    pass_(p)
                pass_(3)

        @block.vector
        def _(dve):
            step = Steps(dve, dve_step)
            V = nc.vector

            def route_parts(j, par, sc, at):
                n = [0]

                def r(ins):
                    n[0] += 1
                    ins.then_inc(route_step, 1)
                    dve.wait_ge(route_step, j * RSTEPS + n[0])

                def top16(v, ix, src, tmp):
                    for f in (lambda: V.max(v[:, 0:8], src), lambda: V.max_index(ix[:, 0:8], v[:, 0:8], src),
                              lambda: V.match_replace(tmp, v[:, 0:8], src, -3e38),
                              lambda: V.max(v[:, 8:16], tmp), lambda: V.max_index(ix[:, 8:16], v[:, 8:16], tmp)):
                        dve.sem_inc(waited, 1)
                        r(f())

                def part(i):
                    n[0] = ROUTE_N[i]
                    if i == 0:
                        r(V.tensor_copy(RS, sc[:, bass.ds(at, 2 * NKEYS)]))
                    if i < 2:
                        top16(RV[:, i, :], RI[:, i * TOPK:(i + 1) * TOPK], RS[:, i * NKEYS:(i + 1) * NKEYS],
                              RS2[:, i * NKEYS:(i + 1) * NKEYS])
                    if i == 2:
                        r(V.tensor_copy(RIF, RI))
                        r(V.tensor_scalar(RIF[:, 0:TOPK], RIF[:, 0:TOPK], float(NKEYS), None, ALU.mult))
                        c = 0
                        for i0, rows_, w in CAND_ROWS:
                            for dst, s1, s2 in ((RC, RV[:, 0, :], RV[:, 1, :]),
                                                (RCI, RIF[:, 0:TOPK], RIF[:, TOPK:2 * TOPK])):
                                r(V.tensor_tensor(dst[:, c:c + rows_ * w].rearrange("p (a b) -> p a b", a=rows_),
                                                  s1[:, i0:i0 + rows_].unsqueeze(2).to_broadcast([P, rows_, w]),
                                                  s2[:, 0:w].unsqueeze(1).to_broadcast([P, rows_, w]), ALU.add))
                            c += rows_ * w
                    if i == 3:
                        top16(RT, RP, RC, RC2)
                        r(V.tensor_scalar(RM, RT[:, 0:1], -1.0, None, ALU.mult))
                        dve.sem_inc(logit_ready, 1)
                    if i == 4:
                        r(V.tensor_copy(RPF, RP))
                        r(V.tensor_tensor(REQ, iota.unsqueeze(1).to_broadcast([P, TOPK, NCAND]),
                                          RPF.unsqueeze(2).to_broadcast([P, TOPK, NCAND]), ALU.is_equal))
                        r(V.tensor_tensor(REQ, REQ, RCI.unsqueeze(1).to_broadcast([P, TOPK, NCAND]), ALU.mult))
                        r(V.tensor_reduce(RX, REQ, AX, ALU.add))
                        r(V.tensor_copy(idxs[:, par, :], RX))
                        dve.sem_inc(idx_ready, 1)
                    if i == 5:
                        dve.wait_ge(expo_ready, j + 1)
                        r(V.reciprocal(RR, RSUM))
                        if not (isinstance(j, int) and j == 0):
                            dve.wait_ge(v_done, (j - 1) * TOPK + V0)
                        r(V.tensor_scalar(gws[:, par, :], RE, RR, None, ALU.mult))
                        dve.sem_inc(gw_ready, 1)
                    assert n[0] == ROUTE_N[i + 1], n
                return part

            sizes = [6, 5, 2 + 2 * len(CAND_ROWS), 6, 5, 2]
            ROUTE_N = [sum(sizes[:i]) for i in range(7)]
            RSTEPS = ROUTE_N[6]

            def route(j):
                part = route_parts(j, j % 2, SC[j // PH], j % PH * 2 * NKEYS)
                for i in range(6):
                    part(i)

            def dot(n, k, par, bufs, sems, count, hc):
                b = (par * TOPK + k) % len(bufs)
                dve.wait_ge(sems[b], count)
                dve.wait_ge(u_done, n - 1 + U0)
                V.tensor_tensor_reduce(out=SCR[k % 2], in0=bufs[b][:, 0:D], in1=hc, scale=1.0, scalar=0.0,
                                       op0=ALU.mult, op1=ALU.add, accum_out=apre[:, par, k:k + 1]).then_inc(u_done, 1)

            def static_slot(n):
                t, j, k = n // TSLOT, n // TOPK, n % TOPK
                dot(n, k, j % 2, GA, ga_in, 16 * (n // NGA + 1), H2[t])
                if n % TSLOT:
                    v_row(n - 1)
                if k in ROUTE_AT and j % PH < PH - 1:
                    i = j + 1
                    route_parts(i, i % 2, SC[t], i % PH * 2 * NKEYS)(ROUTE_AT[k])

            def v_row(n):
                dve.wait_ge(w_done, n + 1)
                if n % TSLOT:
                    dve.wait_ge(v_done, n + V0)
                V.scalar_tensor_tensor(PL[:, :], GA[n % NGA][:, D:2 * D], wexp[:, n // TOPK % 2, n % TOPK:n % TOPK + 1],
                                       PL[:, :], ALU.mult, ALU.add).then_inc(v_done, 1)

            beside = Beside(static_slot, 0)

            def group(name):
                beside.before(name)
                return wait_full(dve, name)

            dve.wait_ge(small_in, 64)
            lg = CO[:, C_LB:C_LB + 16].rearrange("p (d l h) -> p d l h", d=2, l=2)
            step(V.tensor_tensor(LB[:, :, 4, :], lg[:, :, 0], lg[:, :, 1], ALU.max))
            for l in range(2):
                step(V.tensor_tensor(LB[:, :, l, :], lg[:, :, l], LB[:, :, 4, :], ALU.subtract))
            dve.sem_inc(lbx_ready, 1)
            dve.wait_ge(lbe_ready, 1)
            step(V.tensor_tensor(LB[:, :, 4, :], LB[:, :, 2, :], LB[:, :, 3, :], ALU.add))
            step(V.reciprocal(LB[:, :, 5, :], LB[:, :, 4, :]))
            step(V.tensor_tensor(LB[:, :, 0, :], LB[:, :, 2, :], LB[:, :, 5, :], ALU.mult))
            step(V.tensor_scalar(LB[:, :, 1, :], LB[:, :, 0, :], -1.0, 1.0, ALU.mult, ALU.add))

            def ssq(x, t, junk):
                step(V.tensor_tensor_reduce(out=junk, in0=x, in1=x, scale=1.0, scalar=0.0, op0=ALU.mult, op1=ALU.add,
                                            accum_out=st[:, t:t + 1]))
                step(V.tensor_scalar(st[:, 8 + t:9 + t], st[:, t:t + 1], 1.0 / D, EPS, ALU.mult, ALU.add), ssq_ready)

            def normed(n, x, xn):
                dve.wait_ge(rms_ready, n + 1)
                step(V.reciprocal(st[:, 24:25], st[:, 16 + n % NT:17 + n % NT]))
                step(V.tensor_scalar(xn, x, st[:, 24:25], None, ALU.mult), xn_ready)

            def x0(t):
                return XP[:, :] if t == 0 else XL[:, t - 1, :]

            def row(n):
                ps = group(("ada", n))
                if n >= 2:
                    wait_full(dve, ("mod", n - 2))
                step(V.tensor_tensor(GR[n % 2], ps[0:2, 0:SC_W],
                                     BR[:, ADA_SEGS[n // 4], (n % 4) * SC_W:(n % 4 + 1) * SC_W], ALU.add),
                     *freed(("ada", n)), grow_ready)

            row(0)
            for n in range(NADA):
                if n + 1 < NADA:
                    row(n + 1)
                s, q = ADA_SEGS[n // 4], n % 4
                if s not in GATE_SEGS:
                    ps = group(("mod", n))
                    step(V.tensor_copy(ADA[:, {1: 0, 0: 1, 3: 2, 4: 3}[s], :, 2 * q:2 * q + 2],
                                       ps[:, 0:4].rearrange("p (m c) -> p c m", c=2)), *freed(("mod", n)))
                if q == 3 and s in (1, 4):
                    which, col, at = (0, C_N1, 0) if s == 1 else (1, C_N2, 3)
                    for c in range(2):
                        step(V.scalar_tensor_tensor(AM[:, which, c, :], ADA[:, at, c, :], 1.0, CO[:, col:col + 8],
                                                    ALU.add, ALU.mult))
                    dve.sem_inc(am_ready, 1)
                if n == 5:
                    dve.wait_ge(x_in, 32)
                if 6 <= n < 6 + NT:
                    ssq(x0(n - 6), n - 6, SQ1)
            dve.sem_inc(am_ready, 1)
            for t in range(NT):
                if t >= 2:
                    wait_full(dve, ("xT", t - 2))
                normed(t, x0(t), XN1[:, t % 2, :])
            dve.wait_ge(misc_in, 48)
            step(V.tensor_copy(MK[:], MK4), mk_ready)
            def forget(d, latent):
                dve.wait_ge(sig_ready, 8 * latent + 4 * d + 4)
                for h in range(HA):
                    part = FU(d, 1 + h) if latent else FU(d, 0)[:, h * P:(h + 1) * P]
                    step(V.tensor_scalar(part, part, LB[:, d, 1, h:h + 1], LB[:, d, 0, h:h + 1], ALU.mult, ALU.add))
                dve.sem_inc(f_ready, 1)

            for d in range(2):
                forget(d, 0)
            dve.wait_ge(q_ready, 4)

            def out_gate(t):
                dve.wait_ge(win_ready[W_AG], NT + t + 1 if t else 2)
                step(V.tensor_tensor(OA(t), OA(t), anorm, ALU.mult))

            out_gate(0)

            def mul(o, a, b):
                return V.tensor_tensor(o, a, b, ALU.mult)

            step(V.tensor_scalar(ast[:, 160:168], sink, -1.0, None, ALU.mult))
            HS3 = HS.rearrange("p (b n) -> p b n", b=4)

            def take(name, m):
                ps = group(name)
                step(V.copy_predicated(HS3, MK[:, m, :].unsqueeze(1).to_broadcast([P, 4, P]),
                                       ps[:, 0:512].rearrange("p (b n) -> p b n", b=4)), *freed(name))

            def scan(u):
                if u:
                    wait_full(dve, ("ss", 0, 2 * PH - 1) if u == 1 else ("oA", u - 1))
                if u == 1:
                    dve.wait_ge(rope_ready, 4)
                step(V.tensor_scalar(HK[0], FU(0, u), -1.0, 1.0, ALU.mult, ALU.add))
                step(mul(HQ[0], QU(u), FU(0, u)), hg_ready[0])
                take(("diag", u), 14)
                for l in range(LEVELS):
                    group(("lvl", u, l, 0))
                    for ins in half_update(0, l, mul, u):
                        step(ins)
                    dve.sem_inc(hg_ready[0], 1)
                    take(("lvl", u, l, 0), l)
                    take(("lvl", u, l, 1), 7 + l)
                dve.sem_inc(hs_ready, 1)
                dve.wait_ge(hg_ready[1], (LEVELS + 1) * (u + 1))
                ps = group(("dS", u))
                if u == 0:
                    step(V.tensor_copy(NST[0], ps[:, 0:512]))
                    step(V.tensor_copy(NST[1], ps[:, 512:1024]), *freed(("dS", u)), nst_ready, st_ready)
                else:
                    for d in range(2):
                        tot = HT[d][(LEVELS - 1) % 2]
                        for n in range(3):
                            b = n if d == 0 else 3 - n
                            s0 = ST0[:, d, u - 1, :] if n == 0 else HST[:, d, n - 1, :]
                            step(V.scalar_tensor_tensor(HST[:, d, n, :], s0, tot[:, b:b + 1],
                                                        ps[:, (4 * d + b) * P:(4 * d + b + 1) * P], ALU.mult, ALU.add))
                    for x in freed(("dS", u)) + [st_ready]:
                        dve.sem_inc(x, 1)
                beside.before(("oA", u))
                ps = psum(("oA", u))
                dve.wait_ge(osq_ready, u + 1)
                step(V.tensor_reduce(hst[:, 8:12], HSQ.rearrange("p (b n) -> p b n", b=4), AX, ALU.add))
                step(V.tensor_scalar(hst[:, 0:4], hst[:, 8:12], 1.0 / P, EPS, ALU.mult, ALU.add), ossq_ready)
                dve.wait_ge(orms_ready, u + 1)
                step(V.reciprocal(hst[:, 12:16], hst[:, 4:8]))
                for b in range(4):
                    t, h = unit_block(u, b)
                    o = OA(t)[:, h * P:(h + 1) * P]
                    step(V.scalar_tensor_tensor(o, ps[:, b * P:(b + 1) * P], hst[:, 12 + b:13 + b], o,
                                                ALU.mult, ALU.mult))
                for x in freed(("oA", u)) + [oa_ready]:
                    dve.sem_inc(x, 1)

            def attention(tiles):
                SM, _, PT = ATT[tiles[0] > 0]
                beside.before(("sc", tiles[0] * HB))
                dve.wait_ge(qkT_ready, tiles[-1] + 1)
                lo_, hi_ = tiles[0] * HB, (tiles[-1] + 1) * HB

                def row_max(n):
                    t, h = HEADS[n]
                    lo, hi = score_span(t)
                    ps = group(("sc", n))
                    if n >= lo_ + 2:
                        dve.wait_ge(p_ready, n - 1)
                    step(V.tensor_tensor_reduce(out=SM[:, n % 2, lo:hi], in0=ps[:, lo:hi], in1=mbias[:, lo:hi],
                                                scale=1.0, scalar=NEG, op0=ALU.add, op1=ALU.max,
                                                accum_out=ast[:, n:n + 1]), *freed(("sc", n)))
                    step(V.tensor_scalar(ast[:, 40 + n:41 + n], ast[:, n:n + 1], -SCALE, ast[:, 160 + h:161 + h],
                                         ALU.mult, ALU.min), sm_ready)

                def copy_pT(n):
                    lo, hi = score_span(HEADS[n][0])
                    ps = group(("pT", n))
                    step(V.tensor_copy(PT[:, n % 2, lo:hi], ps[:, lo:hi]), *freed(("pT", n)), pT_ready)

                def out_b(t):
                    beside.before(("oB", t))
                    dve.wait_ge(p_ready, HB * (t + 1))
                    s = slice(80 + HB * t, 88 + HB * t)
                    step(V.tensor_tensor(ast[:, s], ast[:, s], ast[:, 120 + HB * t:128 + HB * t], ALU.add))
                    step(V.reciprocal(ast[:, s], ast[:, s]))
                    ps = wait_full(dve, ("oB", t))
                    step(V.tensor_tensor(BQ(t).rearrange("p (h d) -> p h d", h=HB),
                                         ps.rearrange("p (h d) -> p h d", h=HB),
                                         ast[:, s].unsqueeze(2).to_broadcast([P, HB, HD]), ALU.mult),
                         *freed(("oB", t)), ob_ready)

                for n in range(lo_, hi_ + 2):
                    if n < hi_:
                        row_max(n)
                    if lo_ <= n - 1 < hi_:
                        copy_pT(n - 1)
                    if n - 2 >= lo_ and (n - 2) % HB == HB - 1:
                        out_b((n - 2) // HB)

            def post(b):
                tiles, N = BATCHES[b], NB[b]
                for q in range(4):
                    for m in range(2):
                        n = 2 * q + m
                        for a, name in enumerate(("ra", "rb")):
                            ps = group((name, b, n))
                            dve.wait_ge(sig2_ready, 16 * b + 4 * q + 2 * a + m + 1)
                            dst = SAB[b][a][:, m, :]
                            step(V.tensor_tensor(dst, ps[:, 0:N], dst, ALU.mult), *freed((name, b, n)))
                        step(V.tensor_tensor(MT[b][:, n, :], SAB[b][0][:, m, :], SAB[b][1][:, m, :], ALU.add), m_ready)
                if b == 0:
                    dve.wait_ge(gate_ready, 8)
                else:
                    dve.wait_ge(xr_in, 16 if b == 1 else 64)
                for q in range(4):
                    for t in tiles:
                        cs = slice(q * SC_W, (q + 1) * SC_W)
                        ps = group(("y", q, t))
                        gate = (G1P if t == 0 else G1L)[:, cs]
                        step(V.tensor_tensor(SQ2[b][:, 0:SC_W], ps[:, 0:SC_W], gate, ALU.mult), *freed(("y", q, t)))
                        step(V.tensor_tensor(X1[t][:, cs], X1[t][:, cs], SQ2[b][:, 0:SC_W], ALU.add))
                for t in tiles:
                    ssq(X1[t], t, SQ2[b])
                for i, t in enumerate(tiles):
                    beside.before(("x2T", t))
                    if i:
                        wait_full(dve, ("x2T", t - 1))
                    normed(NT + t, X1[t], XN2[b])
                for m in range(2 * PH):
                    ps = group(("ss", b, m))
                    for i, t in enumerate(tiles):
                        step(V.tensor_copy(SC[t][:, m * NKEYS:(m + 1) * NKEYS], ps[:, i * P:(i + 1) * P]))
                    for x in freed(("ss", b, m)):
                        dve.sem_inc(x, 1)

            def tile_end(t):
                dve.wait_ge(u_done, (t + 1) * TSLOT + U0)
                if t < 2:
                    v_row((t + 1) * TSLOT - 1)
                    dve.wait_ge(v_done, (t + 1) * TSLOT + V0)
                else:
                    dve.wait_ge(acc_closed, t - 1)
                step(V.tensor_tensor(SCR[0], PL[:, :], G2[:, 0 if t == 0 else 1, :], ALU.mult), acc_read)
                step(V.tensor_tensor(X1[t], X1[t], SCR[0], ALU.add))
                step(V.tensor_tensor_reduce(out=SCR[0], in0=X1[t], in1=X1[t], scale=1.0, scalar=0.0,
                                            op0=ALU.mult, op1=ALU.add, accum_out=st[:, 28:29]))
                step(V.tensor_scalar(st[:, 29:30], st[:, 28:29], 1.0 / D, EPS, ALU.mult, ALU.add), fss_ready)
                dve.wait_ge(frt_ready, t + 1)
                step(V.reciprocal(st[:, 31:32], st[:, 30:31]))
                dve.wait_ge(nf_in, 16 * (t + 1))
                step(V.scalar_tensor_tensor(X1[t], X1[t], st[:, 31:32], SCR[1], ALU.mult, ALU.mult), y_ready)

            scan(0)
            attention([0])
            post(0)
            dve.wait_ge(h2_ready, 1)
            dve.sem_inc(u_done, U0)
            step(V.memset(PL[:, :], 0.0))
            route(0)
            beside.open(0)
            for d in range(2):
                beside.before(("winT", WIN_T[1 + d], 3))
                forget(d, 1)
            for t in range(1, NT):
                beside.before(("win", W_AG, 1, t))
                out_gate(t)
            dve.wait_ge(q_ready, 8)
            for u in range(1, NT):
                scan(u)
            attention([1, 2, 3, 4])
            post(1)
            beside.rest()
            dve.wait_ge(h2_ready, 2)
            route(PH)
            tile_end(0)
            step(V.memset(PL[:, :], 0.0))
            beside.open(1)
            post(2)
            beside.rest()
            dve.wait_ge(h2_ready, NT)
            route(2 * PH)
            tile_end(1)
            for t in range(2, NT):
                def pass_(p, last):
                    for h in range(2):
                        j = t * PH + p * 2 + h
                        if last and h:
                            nxt = route_parts(j + 1, 0, SC[t + 1], 0) if t + 1 < NT else None
                        else:
                            nxt = route_parts(j + 1, 1 - h, SC[t], (p * 2 + h + 1) * 2 * NKEYS)
                        for k in range(TOPK):
                            i = h * TOPK + k
                            dot(j * TOPK + k, k, h, GB_, gb_in,
                                16 * ((t - 2) * TSLOT // NGB) + p * (16 * HSLOTS // NGB) + 16 * (i // NGB + 1), H2[t])
                            if k in ROUTE_AT and nxt:
                                nxt(ROUTE_AT[k])

                with dve.Fori(0, 3) as p:
                    pass_(p, False)
                pass_(3, True)
                tile_end(t)


def shape_constants():
    f = np.float32
    i = np.arange(P)
    ident = np.eye(P, dtype=f)
    left = np.where(i[None, :] >= i[:, None], 0.0, NEG).astype(f)
    right = np.where(i[None, :] <= i[:, None], 0.0, NEG).astype(f)
    mbias = np.concatenate([left, np.zeros((P, 3 * P), f), right], axis=1)
    pos = np.arange(LAT)
    nf = HD // 4
    inv = f(10000.0) ** (-np.arange(nf, dtype=f) / f(nf))
    ang = [(a.astype(f)[:, None] * inv[None, :]).astype(f) for a in (pos // 64, pos % 64)]
    cos = np.concatenate([np.cos(a) for a in ang for _ in range(2)], axis=1).astype(f)
    sin = np.concatenate([x for a in ang for x in (-np.sin(a), np.sin(a))], axis=1).astype(f)
    lay = lambda a: a.reshape(NT - 1, P, HD).transpose(1, 0, 2).reshape(P, -1)
    iota = np.broadcast_to(np.arange(NCAND, dtype=f), (P, NCAND))
    consts = np.concatenate([ident, mbias, iota, lay(cos), lay(sin)], axis=1)
    masks = np.zeros((P, 15, P), f)
    s, t = i[:, None], i[None, :]
    for l in range(LEVELS):
        same = (s >> (l + 1)) == (t >> (l + 1))
        masks[:, l] = same & ((s >> l) % 2 == 0) & ((t >> l) % 2 == 1)
        masks[:, 7 + l] = same & ((s >> l) % 2 == 1) & ((t >> l) % 2 == 0)
    masks[:, 14] = s == t
    sel = np.zeros((2, 2, P), f)
    sel[0, 0] = 1
    sel[1, 1] = 1
    return consts, masks, sel


_OUTS = [(1, P, D), (1, LAT, D), (1, 1, 2, HA, P, P), (1, 1, P, GB, HD), (1, 1, P, GB, HD)]


def kernel(x_prompt, x_sample, state_hgrn, cache_k, cache_v, c, c_ctx, w_ada, b_ada, norm1, norm2, w_in, lb_logits,
           a_norm, b_sink, w_oa, w_ob, w_out, p_wq, p_keys, p_u, p_v, norm_f):
    import concourse.bacc as _bacc
    from concourse import mybir as _mybir
    from concourse.bass_utils import run_bass_kernel_spmd as _run

    a = np.asarray
    spread = lambda v: np.broadcast_to(a(v).reshape(1, -1), (P, a(v).size))
    consts, masks, sel = shape_constants()
    b = a(b_ada)[0].reshape(6, D)
    arrays = {
        "x_prompt": a(x_prompt)[0], "x_sample": a(x_sample)[0],
        "cols": np.concatenate([a(c_ctx).reshape(-1, P), a(c).reshape(-1, P), a(b_ada).reshape(-1, P),
                                a(norm1).reshape(-1, P), a(norm2).reshape(-1, P), a(lb_logits).reshape(-1, P)]).T,
        "rows": np.concatenate([spread(a_norm), spread(b_sink)], axis=1),
        "normf_rows": spread(norm_f),
        "brow": np.stack([b, b]),
        "consts": consts, "masks": masks, "sel": sel,
        "w_ada": a(w_ada)[0], "w_in": a(w_in)[0], "w_oa": a(w_oa)[0], "w_ob": a(w_ob)[0], "w_out": a(w_out)[0],
        "w_pq": a(p_wq)[0],
        "keysT": a(p_keys)[0].reshape(2 * PH, NKEYS, P).transpose(2, 0, 1).reshape(P, -1),
        "uv": np.concatenate([a(p_u)[0], a(p_v)[0]], axis=1),
        "state": a(state_hgrn)[0, 0],
        "ckT": a(cache_k)[0, 0].reshape(256, GB * HD).T,
        "cv": a(cache_v)[0, 0].reshape(256, GB * HD),
    }
    arrays = {k: np.ascontiguousarray(v) for k, v in arrays.items()}
    nc = _bacc.Bacc("TRN2", target_bir_lowering=False, num_devices=1)
    args = [nc.dram_tensor(f"in_{k}", v.shape, _mybir.dt.from_np(v.dtype), kind="ExternalInput").ap()
            for k, v in arrays.items()]
    outs = [nc.dram_tensor(f"out_{i}", s, _mybir.dt.float32, kind="ExternalOutput").ap() for i, s in enumerate(_OUTS)]
    build(nc, *args, outs[0][0], outs[1][0], outs[2][0, 0], outs[3][0, 0].rearrange("s g d -> s (g d)"),
          outs[4][0, 0].rearrange("s g d -> s (g d)"))
    r = _run(nc, [{f"in_{k}": v for k, v in arrays.items()}], core_ids=[0])
    return tuple(r.results[0][f"out_{i}"] for i in range(len(_OUTS)))
```
